# Optimizing a Trainium2 kernel written in Bass

```python
import jax, jax.numpy as jnp
from jax import lax
import numpy as np

D_MODEL = 2048
BATCH = 1
SEQ = 256
DEPTH = 2

N_MIXERS = 2
N_ATTN_LAYERS = (DEPTH + N_MIXERS - 1) // N_MIXERS
N_POOL_LAYERS = DEPTH // N_MIXERS
HEAD_DIM = 64
N_HEADS = D_MODEL // HEAD_DIM
N_KV_HEADS = N_HEADS // 8
GQA_GROUP = N_HEADS // N_KV_HEADS
WINDOW = 128
BLOCK = WINDOW
N_BUCKETS = 32
MAX_DISTANCE = 128
POOL_WINDOWS = (2, 4, 8, 16)
N_POOL_GROUPS = len(POOL_WINDOWS)
POOL_GROUP_DIM = D_MODEL // N_POOL_GROUPS
D_FF = 5632
CONV_WIDTH = 3
EPS = 1e-6
NEG_INF = -1e30

kernel_name = "hybrid_swa_sink_pool_convffn"

def rmsnorm(x, gain):
    xf = x.astype(jnp.float32)
    y = xf * lax.rsqrt(jnp.mean(xf * xf, axis=-1, keepdims=True) + EPS)
    return (y * gain.astype(jnp.float32)).astype(x.dtype)

def _t5_band_buckets():
    i = np.arange(BLOCK)[:, None]
    j = np.arange(2 * BLOCK)[None, :]
    n = np.maximum(BLOCK + i - j, 0)
    max_exact = N_BUCKETS // 2
    nf = np.maximum(n, 1).astype(np.float32)
    large = max_exact + (np.log(nf / max_exact) / np.log(MAX_DISTANCE / max_exact)
                         * (N_BUCKETS - max_exact)).astype(np.int32)
    large = np.minimum(large, N_BUCKETS - 1)
    return np.where(n < max_exact, n, large).astype(np.int32)

def _band_mask(n_blocks):
    i = np.arange(BLOCK)[:, None]
    j = np.arange(2 * BLOCK)[None, :]
    dist = BLOCK + i - j
    in_win = (dist >= 0) & (dist < WINDOW)
    key_pos = np.arange(n_blocks)[:, None, None] * BLOCK - BLOCK + j[None]
    return in_win[None] & (key_pos >= 0)

def sliding_window_attention(h, w_qkv, q_gain, k_gain, sinks, rel_bias, w_o):
    B, S, _ = h.shape
    nb = S // BLOCK
    qkv = h @ w_qkv
    q, k, v = jnp.split(qkv, [N_HEADS * HEAD_DIM, (N_HEADS + N_KV_HEADS) * HEAD_DIM], axis=-1)
    q = rmsnorm(q.reshape(B, S, N_HEADS, HEAD_DIM), q_gain)
    k = rmsnorm(k.reshape(B, S, N_KV_HEADS, HEAD_DIM), k_gain)
    v = v.reshape(B, S, N_KV_HEADS, HEAD_DIM)
    q = q.reshape(B, nb, BLOCK, N_KV_HEADS, GQA_GROUP, HEAD_DIM)

    def band(t):
        t = t.reshape(B, nb, BLOCK, N_KV_HEADS, HEAD_DIM)
        prev = jnp.pad(t[:, :-1], ((0, 0), (1, 0), (0, 0), (0, 0), (0, 0)))
        return jnp.concatenate([prev, t], axis=2)

    kb, vb = band(k), band(v)
    s = jnp.einsum('bnqkgd,bnskd->bnkgqs', q, kb).astype(jnp.float32) * (HEAD_DIM ** -0.5)
    bias = rel_bias[:, _t5_band_buckets()].astype(jnp.float32)
    bias = bias.reshape(N_KV_HEADS, GQA_GROUP, BLOCK, 2 * BLOCK)
    mask = jnp.asarray(_band_mask(nb))[None, :, None, None]
    s = jnp.where(mask, s + bias, NEG_INF)
    sink = sinks.astype(jnp.float32).reshape(N_KV_HEADS, GQA_GROUP)[:, :, None, None]
    m = jnp.maximum(jnp.max(s, axis=-1, keepdims=True), sink)
    p = jnp.exp(s - m)
    p = p / (jnp.sum(p, axis=-1, keepdims=True) + jnp.exp(sink - m))
    o = jnp.einsum('bnkgqs,bnskd->bnqkgd', p.astype(vb.dtype), vb)
    return o.reshape(B, S, N_HEADS * HEAD_DIM) @ w_o

def multiscale_pool_mixer(h, w_pool, scale):
    B, S, _ = h.shape
    hg = h.reshape(B, S, N_POOL_GROUPS, POOL_GROUP_DIM)
    hf = hg.astype(jnp.float32)
    c = jnp.cumsum(hf, axis=1)
    t = jnp.arange(S)
    means = []
    for g, w in enumerate(POOL_WINDOWS):
        cg = c[:, :, g]
        lag = jnp.pad(cg, ((0, 0), (w, 0), (0, 0)))[:, :S]
        cnt = jnp.minimum(t + 1, w).astype(jnp.float32)[None, :, None]
        means.append((cg - lag) / cnt)
    d = (jnp.stack(means, axis=2) - hf).astype(h.dtype)
    y = jnp.einsum('bsgc,gce->bsge', d, w_pool).reshape(B, S, D_MODEL)
    return y * scale

def conv_gated_mlp(h, w_up, conv_w, conv_b, w_down):
    S = h.shape[1]
    u = h @ w_up
    up = jnp.pad(u, ((0, 0), (CONV_WIDTH - 1, 0), (0, 0)))
    u = sum(conv_w[k] * up[:, k:k + S] for k in range(CONV_WIDTH)) + conv_b
    gate, val = jnp.split(u, 2, axis=-1)
    return (jax.nn.silu(gate) * val) @ w_down

def setup_inputs(seed: int = 0) -> dict:
    key = jax.random.key(seed)
    ks = jax.random.split(key, 16)
    f32 = jnp.float32
    qkv_out = (N_HEADS + 2 * N_KV_HEADS) * HEAD_DIM
    return {
        "x": jax.random.normal(ks[0], (BATCH, SEQ, D_MODEL), f32),
        "norm_mix": 1.0 + 0.05 * jax.random.normal(ks[1], (DEPTH, D_MODEL), f32),
        "norm_ffn": 1.0 + 0.05 * jax.random.normal(ks[2], (DEPTH, D_MODEL), f32),
        "rel_bias": 0.5 * jax.random.normal(ks[3], (N_HEADS, N_BUCKETS), f32),
        "attn_w_qkv": jax.random.normal(ks[4], (N_ATTN_LAYERS, D_MODEL, qkv_out), f32) * D_MODEL ** -0.5,
        "attn_q_gain": 1.0 + 0.05 * jax.random.normal(ks[5], (N_ATTN_LAYERS, HEAD_DIM), f32),
        "attn_k_gain": 1.0 + 0.05 * jax.random.normal(ks[6], (N_ATTN_LAYERS, HEAD_DIM), f32),
        "attn_sinks": 0.5 * jax.random.normal(ks[7], (N_ATTN_LAYERS, N_HEADS), f32),
        "attn_w_o": jax.random.normal(ks[8], (N_ATTN_LAYERS, N_HEADS * HEAD_DIM, D_MODEL), f32) * (N_HEADS * HEAD_DIM) ** -0.5,
        "pool_w": jax.random.normal(ks[9], (N_POOL_LAYERS, N_POOL_GROUPS, POOL_GROUP_DIM, POOL_GROUP_DIM), f32) * POOL_GROUP_DIM ** -0.5,
        "pool_scale": 1.0 + 0.05 * jax.random.normal(ks[10], (N_POOL_LAYERS, D_MODEL), f32),
        "ffn_w_up": jax.random.normal(ks[11], (DEPTH, D_MODEL, 2 * D_FF), f32) * D_MODEL ** -0.5,
        "ffn_conv_w": jax.random.normal(ks[12], (DEPTH, CONV_WIDTH, 2 * D_FF), f32) * CONV_WIDTH ** -0.5,
        "ffn_conv_b": 0.02 * jax.random.normal(ks[13], (DEPTH, 2 * D_FF), f32),
        "ffn_w_down": jax.random.normal(ks[14], (DEPTH, D_FF, D_MODEL), f32) * D_FF ** -0.5,
    }

def reference(x, norm_mix, norm_ffn, rel_bias, attn_w_qkv, attn_q_gain, attn_k_gain,
              attn_sinks, attn_w_o, pool_w, pool_scale, ffn_w_up, ffn_conv_w, ffn_conv_b,
              ffn_w_down):
    for i in range(DEPTH):
        h = rmsnorm(x, norm_mix[i])
        j = i // N_MIXERS
        if i % N_MIXERS == 0:
            mix = sliding_window_attention(h, attn_w_qkv[j], attn_q_gain[j], attn_k_gain[j],
                                           attn_sinks[j], rel_bias, attn_w_o[j])
        else:
            mix = multiscale_pool_mixer(h, pool_w[j], pool_scale[j])
        x = x + mix
        h = rmsnorm(x, norm_ffn[i])
        x = x + conv_gated_mlp(h, ffn_w_up[i], ffn_conv_w[i], ffn_conv_b[i], ffn_w_down[i])
    return x


_drawn_inputs = setup_inputs


def setup_inputs(seed=0):
    import zlib

    import numpy as np

    out = dict(_drawn_inputs(seed))
    spreads = {}
    factors = {'attn_q_gain': 4.557, 'attn_k_gain': 4.439, 'attn_sinks': 26.7, 'ffn_conv_b': 3.003}
    for name, (base, spread) in spreads.items():
        noise = np.random.default_rng([zlib.crc32(name.encode()), seed]).standard_normal(out[name].shape)
        drawn = base * np.exp(spread * noise) if base else spread * noise
        out[name] = __import__('jax').numpy.asarray(drawn.astype(out[name].dtype))
    for name, factor in factors.items():
        out[name] = (out[name] * factor).astype(out[name].dtype)
    return out
```

```python
from contextlib import ExitStack

import concourse.bass as bass
from concourse import mybir

F32 = mybir.dt.float32
F32R = mybir.dt.float32r
I32 = mybir.dt.int32
ALU = mybir.AluOpType
ACT = mybir.ActivationFunctionType
AX = mybir.AxisListType
ds = bass.ds

P = 128
SLOTS = 4
UNIT_K = 4
UNIT_N = 512
POOL_WINDOWS = (2, 4, 8, 16)
EPS = 1e-6
RSQRT_SEED = 0x5F3759DF
RSQRT_STEPS = 12
MASKED = -1e30
BIAS_ROW = 3 * P


def build_trunk(nc, x_in, norm_mix, norm_ffn, rel_bias, w_qkv, q_gain, k_gain, sinks, w_o, w_pool,
                pool_scale, w_up, conv_w, conv_b, w_down, bucket_onehot, inv_count, out):
    T, D = x_in.shape[1], x_in.shape[2]
    DH = q_gain.shape[1]
    NH = sinks.shape[1]
    NB = rel_bias.shape[1]
    NKV = (w_qkv.shape[2] // DH - NH) // 2
    F = w_down.shape[1]
    KC = D // P
    FC = F // P
    TT = T // P
    DG = D // UNIT_N
    FG = F // UNIT_N
    PART = KC // UNIT_K
    WHOLE_PARTS = FG // PART
    LAST_PART = FG - WHOLE_PARTS * PART
    assert (T, TT, DG, NKV, KC, LAST_PART) == (256, 2, 4, 4, 16, 3) and NH == 8 * NKV and NH == NB == 32 and 2 * DH == P

    TURN_KV, TURN_Q0, TURN_WO = 0, 1, 1 + NKV
    TURN_FFN = [TURN_WO + DG, 0]
    PART_TURNS = 2 * PART + DG
    FFN_TURNS = WHOLE_PARTS * PART_TURNS + 2 * LAST_PART + DG * LAST_PART // UNIT_K
    TURN_POOL = TURN_FFN[0] + FFN_TURNS
    TURN_FFN[1] = TURN_POOL + 1
    TURNS = TURN_FFN[1] + FFN_TURNS
    PART_GROUPS = 2 * PART + DG
    FFN_GROUPS = WHOLE_PARTS * PART_GROUPS + 2 * LAST_PART + DG
    GROUP_FFN = [DG, DG + FFN_GROUPS + DG]
    GROUP_POOL = DG + FFN_GROUPS
    ITER_FFN = [0, FG]
    X_FFN = [0, (WHOLE_PARTS + 2) * DG]
    X_LAST = [n + WHOLE_PARTS * DG for n in X_FFN]
    X_POOL = (WHOLE_PARTS + 1) * DG

    qkv_v = w_qkv[0].rearrange("(k p) n -> p k n", p=P)
    wo_v = w_o[0].rearrange("(k p) n -> p k n", p=P)
    up_v = [w_up[l].rearrange("(k p) n -> p k n", p=P) for l in range(2)]
    down_v = [w_down[l].rearrange("(k p) n -> p k n", p=P) for l in range(2)]
    pool_v = [w_pool[0, g].rearrange("(k p) n -> p k n", p=P) for g in range(DG)]
    x_v = x_in[0].rearrange("(t p) d -> p t d", p=P)
    out_v = out[0].rearrange("(t p) d -> p t d", p=P)
    bias_rows_dram = nc.dram_tensor("bias_rows_dram", [NH, BIAS_ROW], F32)
    taps_dram = nc.dram_tensor("taps_dram", [P, 2 * 4 * 2 * FC], F32)

    place_at = [(nc.sbuf_base + 31) // 32 * 32]

    def place(name, shape, dt=F32):
        n = 4
        for d in shape[1:]:
            n *= d
        t = nc.alloc_sbuf_tensor_at(name, [P] + list(shape[1:]), dt, offset=place_at[0])
        place_at[0] += (n + 31) // 32 * 32
        return t

    x_t = place("x_t", [P, KC, T])
    h_hl = place("h_hl", [P, KC, 2 * T], F32R)
    g_at = place_at[0]
    g_hl = place("g_hl", [P, KC, 2 * T], F32R)
    raw = place("raw", [P, SLOTS, UNIT_K, UNIT_N])
    w_hi = place("w_hi", [P, SLOTS, UNIT_K, UNIT_N], F32R)
    w_lo = place("w_lo", [P, SLOTS, UNIT_K, UNIT_N], F32R)
    ident = place("ident", [P, P])
    mirror = place("mirror", [P, P])
    gains = place("gains", [P, 5 * KC])
    token_ssq = place("token_ssq", [P, TT])
    token_mean = place("token_mean", [P, 2, TT])
    token_rstd = place("token_rstd", [P, TT])
    q_gain_col = place("q_gain_col", [P, 1])
    k_gain_col = place("k_gain_col", [P, 1])
    neg_sink = place("neg_sink", [P, NH])
    sink = place("sink", [P, NH])
    stage_at = place_at[0]
    x_rows = place("x_rows", [P, TT, D])
    conv_rows = place("conv_rows", [P, 2, 4, P])
    gain_rows = place("gain_rows", [P, P])
    table = place("table", [P, NB])
    table_t = place("table_t", [P, NH])
    table_p = place("table_p", [P, NH])
    onehot = place("onehot", [P, P])
    bias_rows = place("bias_rows", [P, BIAS_ROW])
    taps_early = place("taps_early", [P, 2, 4, 2 * FC])
    place_at[0] = stage_at
    probs = place("probs", [P, 4, 2 * P])
    probs_t = place("probs_t", [P, 2, 4, P])
    q_rows = place("q_rows", [P, TT, UNIT_N])
    q_t = place("q_t", [P, 4, T])
    k_t = place("k_t", [P, NKV, T])
    k_group = place("k_group", [P, 1, T])
    v_rows = place("v_rows", [P, TT, NKV, DH])
    v_group = place("v_group", [P, TT, 1, DH])
    o_rows = place("o_rows", [P, 4, DH])
    bias_b = place("bias_b", [P, 4, 2 * P])
    head_ssq = place("head_ssq", [P, TT, 8])
    head_mean = place("head_mean", [P, 2, TT, 8])
    head_rinv = place("head_rinv", [P, TT, 8])
    row_max = place("row_max", [P, 2, 4])
    neg_max = place("neg_max", [P, 2, 4])
    row_sum = place("row_sum", [P, 2, 4])
    sink_arg = place("sink_arg", [P, 2, 4])
    sink_exp = place("sink_exp", [P, 2, 4])
    row_den = place("row_den", [P, 2, 4])
    row_rinv = place("row_rinv", [P, 2, 4])
    assert place_at[0] <= nc.sbuf_usable_end, (place_at[0], nc.sbuf_usable_end)
    bias_a = nc.alloc_sbuf_tensor_at("bias_a", [P, 4, 2 * P], F32, offset=g_at + (KC - 2) * 2 * T * 4)
    bias_ab = [bias_a, bias_b]
    place_at[0] = stage_at
    tail = place("tail", [P, 4, T])
    pre = place("pre", [P, 4, T])
    y_gate = place("y_gate", [P, 4, T])
    y_val = place("y_val", [P, 4, T])
    squares = place("squares", [P, 4, T])
    ssq_part = place("ssq_part", [P, T])
    ssq_local = place("ssq_local", [P, T])
    ssq_all = place("ssq_all", [P, T])
    ssq_mean = place("ssq_mean", [P, 2, T])
    rstd = place("rstd", [P, T])
    taps = place("taps", [P, 2, 4, 2 * FC])
    pool_inv = place("pool_inv", [P, DG, max(POOL_WINDOWS)])
    assert place_at[0] <= nc.sbuf_usable_end

    with ExitStack() as ctx:
        ps = ctx.enter_context(nc.psum_tensor("ps", [P, 8, UNIT_N], F32))

        def sem(name):
            return ctx.enter_context(nc.semaphore(name))

        raw_landed = [sem(f"raw_landed{s}") for s in range(SLOTS)]
        hi_split, lo_split, units_done = sem("hi_split"), sem("lo_split"), sem("units_done")
        x_landed = [sem(f"x_landed{i}") for i in range(4)]
        params_landed, cols_landed, table_landed = sem("params_landed"), sem("cols_landed"), sem("table_landed")
        table_turned = sem("table_turned")
        ident_zero, ident_ready = sem("ident_zero"), sem("ident_ready")
        params_turned, params_ready = sem("params_turned"), sem("params_ready")
        x_turned, x_copied = sem("x_turned"), sem("x_copied")
        bias_filled, bias_built, bias_stored = sem("bias_filled"), sem("bias_built"), sem("bias_stored")
        bias_landed = [sem("bias_landed_a"), sem("bias_landed_b")]
        ssq_done, rstd_ready, sink_ready = sem("ssq_done"), sem("rstd_ready"), sem("sink_ready")
        h_hi_ready, h_ready = sem("h_hi_ready"), sem("h_ready")
        kv_squared, kv_summed, kv_rinv, k_rows_ready = sem("kv_squared"), sem("kv_summed"), sem("kv_rinv"), sem("k_rows_ready")
        k_turned, k_t_ready = sem("k_turned"), sem("k_t_ready")
        q_squared, q_summed, q_rinv, q_ready = sem("q_squared"), sem("q_summed"), sem("q_rinv"), sem("q_ready")
        q_turned, q_t_ready = sem("q_turned"), sem("q_t_ready")
        k_group_ready, v_group_ready = sem("k_group_ready"), sem("v_group_ready")
        scores_done, biased, maxed, neg_max_ready = sem("scores_done"), sem("biased"), sem("maxed"), sem("neg_max_ready")
        sink_arg_ready, exp_done, den_ready, rinv_ready = sem("sink_arg_ready"), sem("exp_done"), sem("den_ready"), sem("rinv_ready")
        probs_turned, probs_t_act, probs_t_dve = sem("probs_turned"), sem("probs_t_act"), sem("probs_t_dve")
        pv_done, o_ready, o_turned, o_hi, o_lo = sem("pv_done"), sem("o_ready"), sem("o_turned"), sem("o_hi"), sem("o_lo")
        tail_copied, banks_added = sem("tail_copied"), sem("banks_added")
        x_added = sem("x_added")
        squared, ssq_reduced, ssq_local_ready, ssq_all_ready, token_scale = sem("squared"), sem("ssq_reduced"), sem("ssq_local_ready"), sem("ssq_all_ready"), sem("token_scale")
        pre_scaled, tap_mid, tap_prev, conv_done = sem("pre_scaled"), sem("tap_mid"), sem("tap_prev"), sem("conv_done")
        silu_done, gated, g_hi, g_lo = sem("silu_done"), sem("gated"), sem("g_hi"), sem("g_lo")
        taps_landed = sem("taps_landed")
        pool_inv_landed, pool_chain = sem("pool_inv_landed"), sem("pool_chain")
        out_turned, out_copied = sem("out_turned"), sem("out_copied")
        out_stored = [sem("out_stored_even"), sem("out_stored_odd")]

        block = ctx.enter_context(nc.Block())

        @block.sync
        def _(sp):
            for i in range(4):
                w = D // 4
                sp.dma_start(x_rows[:, :, i * w:(i + 1) * w], x_v[:, :, i * w:(i + 1) * w]).then_inc(x_landed[i], 16)

            def load(turn, slot, src, first=False):
                if not first:
                    sp.wait_ge(lo_split, SLOTS * turn + (slot + 1 - SLOTS))
                sp.dma_start(raw[:, slot], src).then_inc(raw_landed[slot], 16)

            for kq in range(4):
                load(TURN_KV, kq, qkv_v[:, 4 * kq:4 * kq + 4, D:D + UNIT_N], first=True)
            with sp.Fori(0, NKV) as g:
                for kq in range(4):
                    load(TURN_Q0 + g, kq, qkv_v[:, 4 * kq:4 * kq + 4, ds(g * UNIT_N, UNIT_N)])
            with sp.Fori(0, DG) as j:
                for kq in range(4):
                    load(TURN_WO + j, kq, wo_v[:, 4 * kq:4 * kq + 4, ds(j * UNIT_N, UNIT_N)])

            def load_up(layer, turn, f):
                for half in range(2):
                    for kq in range(4):
                        load(turn + half, kq, up_v[layer][:, 4 * kq:4 * kq + 4, ds(f * UNIT_N + half * F, UNIT_N)])

            for layer in range(2):
                t0 = TURN_FFN[layer]
                with sp.Fori(0, WHOLE_PARTS) as part:
                    with sp.Fori(0, PART) as i:
                        load_up(layer, t0 + part * PART_TURNS + i * 2, part * PART + i)
                    with sp.Fori(0, DG) as j:
                        for kq in range(4):
                            load(t0 + part * PART_TURNS + (2 * PART + j), kq,
                                 down_v[layer][:, ds(part * KC + 4 * kq, 4), ds(j * UNIT_N, UNIT_N)])
                t1 = t0 + WHOLE_PARTS * PART_TURNS
                with sp.Fori(0, LAST_PART) as i:
                    load_up(layer, t1 + i * 2, i + WHOLE_PARTS * PART)
                for n in range(DG * LAST_PART):
                    j, kq = divmod(n, LAST_PART)
                    k = WHOLE_PARTS * KC + 4 * kq
                    load(t1 + 2 * LAST_PART + n // SLOTS, n % SLOTS,
                         down_v[layer][:, k:k + 4, j * UNIT_N:(j + 1) * UNIT_N])
                if layer == 0:
                    for g in range(DG):
                        load(TURN_POOL, g, pool_v[g])
            for j in range(DG):
                sp.wait_ge(out_copied, j + 1)
                sp.dma_start(out_v[:, :, j * UNIT_N:(j + 1) * UNIT_N],
                             (y_gate if j % 2 == 0 else y_val)[:].rearrange("p a t -> p (a t)").rearrange(
                                 "p (t d) -> p t d", t=TT)).then_inc(out_stored[j % 2], 16)
            for b in range(2):
                sp.wait_ge(out_stored[b], 16 * (DG // 2))

        @block.gpsimd
        def _(pool):
            nc.gpsimd.memset(ident[:], 0.0).then_inc(ident_zero, 1)
            nc.gpsimd.memset(mirror[:], 0.0).then_inc(ident_zero, 1)
            pool.dma_start(gain_rows[0:2 * KC, :], norm_mix.rearrange("l (c p) -> (l c) p", p=P)).then_inc(params_landed, 16)
            pool.dma_start(gain_rows[2 * KC:4 * KC, :], norm_ffn.rearrange("l (c p) -> (l c) p", p=P)).then_inc(params_landed, 16)
            pool.dma_start(gain_rows[4 * KC:5 * KC, :], pool_scale[0].rearrange("(c p) -> c p", p=P)).then_inc(params_landed, 16)
            for l in range(2):
                pool.dma_start(conv_rows[0:2 * FC, l, 0:3, :], conv_w[l].rearrange("k (c p) -> c k p", p=P)).then_inc(params_landed, 16)
            pool.dma_start(conv_rows[0:2 * FC, :, 3, :], conv_b.rearrange("l (c p) -> c l p", p=P)).then_inc(params_landed, 16)
            pool.wait_ge(ident_zero, 2)
            nc.gpsimd.affine_select(out=ident[:], in_=ident[:], compare_op=ALU.not_equal, fill=1.0, base=0,
                                    pattern=[[-1, P]], channel_multiplier=1).then_inc(ident_ready, 1)
            nc.gpsimd.affine_select(out=mirror[:], in_=mirror[:], compare_op=ALU.not_equal, fill=1.0, base=1 - P,
                                    pattern=[[1, P]], channel_multiplier=1).then_inc(ident_ready, 1)
            pool.dma_start(table[0:NH, :], rel_bias).then_inc(table_landed, 16)
            pool.dma_start(onehot[0:NB, :], bucket_onehot).then_inc(table_landed, 16)
            for r in range(2):
                pool.dma_start(q_gain_col[r * DH:(r + 1) * DH, :], q_gain.rearrange("a d -> d a"), allow_slow_non_contiguous=True).then_inc(cols_landed, 16)
                pool.dma_start(k_gain_col[r * DH:(r + 1) * DH, :], k_gain.rearrange("a d -> d a"), allow_slow_non_contiguous=True).then_inc(cols_landed, 16)
            pool.dma_start(sink[:], sinks.broadcast_to([P, NH])).then_inc(cols_landed, 16)
            pool.wait_ge(bias_built, 1)
            pool.dma_start(bias_rows_dram.ap()[:, :], bias_rows[0:NH, :]).then_inc(bias_stored, 16)
            pool.wait_ge(params_ready, 2)
            pool.dma_start(taps_dram.ap()[:, :], taps_early[:].rearrange("p l k c -> p (l k c)")).then_inc(bias_stored, 16)
            pool.wait_ge(bias_stored, 32)

            def load_bias(g, half):
                src = bass.AP(tensor=bias_rows_dram, offset=(g * 8 + 4 * half) * BIAS_ROW,
                              ap=[[1, P], [BIAS_ROW, 4], [1, 2 * P]])
                pool.dma_start(bias_ab[half][:], src).then_inc(bias_landed[half], 16)

            for half in range(2):
                if half == 1:
                    pool.wait_ge(k_rows_ready, TT)
                load_bias(0, half)
            with pool.Fori(1, NKV) as g:
                for half in range(2):
                    pool.wait_ge(biased, 4 * g - 2 + 2 * half)
                    load_bias(g, half)
            pool.wait_ge(biased, 4 * NKV)
            pool.wait_ge(banks_added, 1)
            pool.dma_start(taps[:].rearrange("p l k c -> p (l k c)"), taps_dram.ap()[:, :]).then_inc(taps_landed, 16)
            pool.dma_start(pool_inv[:], inv_count.rearrange("g w -> (g w)").unsqueeze(0).broadcast_to(
                [P, DG * max(POOL_WINDOWS)])).then_inc(pool_inv_landed, 16)
            for n in range(3):
                pool.wait_ge(ssq_local_ready, (DG - 1) * (n + 1))
                if n:
                    pool.wait_ge(token_scale, RSQRT_STEPS * n)
                nc.gpsimd.partition_all_reduce(ssq_all[:], ssq_local[:], P, bass.bass_isa.ReduceOp.add).then_inc(ssq_all_ready, 1)

        @block.scalar
        def _(act):
            def copy_out(j):
                act.wait_ge(out_turned, j + 1)
                if j >= 2:
                    act.wait_ge(out_stored[j % 2], 16 * (j // 2))
                nc.scalar.copy((y_gate if j % 2 == 0 else y_val)[:].rearrange("p a t -> p (a t)"),
                               ps[:, 4 * (j % 2):4 * (j % 2) + 2, :].rearrange("p b n -> p (b n)")).then_inc(out_copied, 1)

            def split_hi(turn, slot, first=False):
                act.wait_ge(raw_landed[slot], 16 * (turn + 1))
                if not first:
                    act.wait_ge(units_done, SLOTS * turn + (slot + 1 - SLOTS))
                nc.scalar.copy(w_hi[:, slot], raw[:, slot]).then_inc(hi_split, 1)

            def write_h_hi(chunks, gain_at):
                for k in chunks:
                    last = nc.scalar.activation(h_hl[:, k, 0:T], x_t[:, k, :], ACT.Identity, scale=gains[:, gain_at + k:gain_at + k + 1])
                last.then_inc(h_hi_ready, 1)

            act.wait_ge(params_ready, 1)
            for j in range(DG):
                act.wait_ge(x_copied, 2 * j + 2)
                write_h_hi(range(4 * j, 4 * j + 4), 0)
                split_hi(TURN_KV, j, first=True)
            for i in range(4):
                act.wait_ge(x_landed[i], 16)
            for tt in range(TT):
                nc.scalar.activation(g_hl[:, 4 * tt:4 * tt + 4, :].rearrange("p c t -> p (c t)"), x_rows[:, tt, :], ACT.Square,
                                     accum_out=token_ssq[:, tt:tt + 1]).then_inc(ssq_done, 1)

            for s in range(SLOTS):
                split_hi(TURN_Q0, s)
            act.wait_ge(rstd_ready, RSQRT_STEPS)
            act.wait_ge(bias_stored, 32)
            act.wait_ge(units_done, SLOTS * TURN_Q0)
            for tt in range(TT):
                nc.scalar.activation(v_rows[:, tt].rearrange("p h d -> p (h d)"), ps[:, 2 + tt, NKV * DH:2 * NKV * DH],
                                     ACT.Identity, scale=token_rstd[:, tt:tt + 1])
                nc.scalar.activation(probs[:, tt, :], ps[:, 2 + tt, 0:NKV * DH], ACT.Square,
                                     scale=token_rstd[:, tt:tt + 1]).then_inc(kv_squared, 1)

            def square_q(g, turn):
                act.wait_ge(units_done, SLOTS * turn + SLOTS)
                for tt in range(TT):
                    nc.scalar.activation(q_rows[:, tt, :], ps[:, tt, :], ACT.Square,
                                         scale=token_rstd[:, tt:tt + 1]).then_inc(q_squared, 1)

            for s in range(SLOTS):
                split_hi(TURN_Q0 + 1, s)
            act.wait_ge(cols_landed, 16 * 5)
            for tt in range(TT):
                act.wait_ge(k_turned, tt + 1)
                nc.scalar.activation(k_t[:, :, tt * P:(tt + 1) * P], ps[:, 4 + tt, :].rearrange("p (h q) -> p h q", h=NKV),
                                     ACT.Identity, scale=k_gain_col[:, 0:1]).then_inc(k_t_ready, 1)
            square_q(0, TURN_Q0)

            def attend(g, turn, last):
                act.wait_ge(k_t_ready, TT)
                nc.scalar.copy(k_group[:], k_t[:, ds(g, 1) if not last else slice(g, g + 1), :]).then_inc(k_group_ready, 1)
                for tt in range(TT):
                    act.wait_ge(q_turned, 2 * g + (tt + 1))
                    nc.scalar.activation(q_t[:, :, tt * P:(tt + 1) * P], ps[:, 7, :].rearrange("p (c q) -> p c q", c=4),
                                         ACT.Identity, scale=q_gain_col[:, 0:1]).then_inc(q_t_ready, 1)

                def exps(s):
                    b, lo = s % 2, P * (1 - s % 2)
                    act.wait_ge(neg_max_ready, 4 * g + (s + 1))
                    for j in range(4):
                        nc.scalar.activation(probs[:, j, lo:], probs[:, j, lo:], ACT.Exp, bias=neg_max[:, b, j:j + 1],
                                             accum_out=row_sum[:, b, j:j + 1])
                    act.wait_ge(sink_arg_ready, 4 * g + (s + 1))
                    nc.scalar.activation(sink_exp[:, b, :], sink_arg[:, b, :], ACT.Exp).then_inc(exp_done, 1)

                def turned_out(s):
                    half, tt = divmod(s, 2)
                    act.wait_ge(o_turned, 4 * g + (s + 1))
                    c0 = 4 * g + 2 * half
                    nc.scalar.copy(g_hl[:, ds(c0, 2) if not last else slice(c0, c0 + 2), tt * P:(tt + 1) * P],
                                   ps[:, 7, 0:2 * P].rearrange("p (c q) -> p c q", c=2)).then_inc(o_hi, 1)

                exps(0)
                for s in range(4):
                    if s:
                        turned_out(s - 1)
                    act.wait_ge(probs_turned, 4 * g + (s + 1))
                    kb = 1 - s % 2
                    nc.scalar.copy(probs_t[:, kb], ps[:, 4 + kb, :].rearrange("p (h q) -> p h q", h=4)).then_inc(probs_t_act, 1)
                    if s < 3:
                        split_hi(turn + 1, s)
                        exps(s + 1)
                if not last:
                    square_q(g, turn)
                turned_out(3)
                split_hi(turn + 1, 3)

            with act.Fori(0, NKV - 1) as g:
                attend(g, TURN_Q0 + 1 + g, False)
            attend(NKV - 1, TURN_WO, True)

            def square_x(group, n):
                if n:
                    act.wait_ge(ssq_reduced, n)
                nc.scalar.activation(squares[:], x_t[:, 4 * group:4 * group + 4, :], ACT.Square).then_inc(squared, 1)

            for j in range(DG):
                if j:
                    for s in range(SLOTS):
                        split_hi(TURN_WO + j + 1, s)
                act.wait_ge(banks_added, j + 1)
                square_x(j, j)
                write_h_hi(range(4 * j, 4 * j + 4), 2 * KC)

            def copy_tail(group, end_unit, banks):
                act.wait_ge(units_done, end_unit)
                act.wait_ge(banks_added, group)
                nc.scalar.copy(tail[:], ps[:, banks:banks + 4, T:2 * T]).then_inc(tail_copied, 1)

            def mlp_group(turn, group, it, chunk0):
                for s in range(SLOTS):
                    split_hi(turn + 1, s)
                copy_tail(group, SLOTS * turn + SLOTS, 0)
                split_hi(turn + 2, 0)
                split_hi(turn + 2, 1)
                act.wait_ge(conv_done, 2 * it + 1)
                nc.scalar.activation(y_gate[:], y_gate[:], ACT.Silu).then_inc(silu_done, 1)
                split_hi(turn + 2, 2)
                split_hi(turn + 2, 3)
                copy_tail(group + 1, SLOTS * turn + 2 * SLOTS, 4)
                act.wait_ge(gated, it + 1)
                nc.scalar.copy(g_hl[:, ds(chunk0, 4), 0:T], y_val[:]).then_inc(g_hi, 1)

            for layer in range(2):
                t0, g0, it0 = TURN_FFN[layer], GROUP_FFN[layer], ITER_FFN[layer]
                with act.Fori(0, WHOLE_PARTS) as part:
                    with act.Fori(0, PART) as i:
                        mlp_group(part * PART_TURNS + i * 2 + t0, part * PART_GROUPS + i * 2 + g0, part * PART + i + it0, i * 4)
                    with act.Fori(0, DG // 2) as j2:
                        for b in range(2):
                            turn = part * PART_TURNS + j2 * 2 + (t0 + 2 * PART + b)
                            for s in range(SLOTS):
                                split_hi(turn + 1, s)
                            copy_tail(part * PART_GROUPS + j2 * 2 + (g0 + 2 * PART + b), SLOTS * turn + SLOTS, 4 * b)
                t1, g1 = t0 + WHOLE_PARTS * PART_TURNS, g0 + WHOLE_PARTS * PART_GROUPS
                with act.Fori(0, LAST_PART) as i:
                    mlp_group(i * 2 + t1, i * 2 + g1, i + (it0 + WHOLE_PARTS * PART), i * 4)
                t2, g2 = t1 + 2 * LAST_PART, g1 + 2 * LAST_PART
                for n in range(DG * LAST_PART):
                    if t2 + 1 + n // SLOTS < TURNS:
                        split_hi(t2 + 1 + n // SLOTS, n % SLOTS)
                    if n % LAST_PART == LAST_PART - 1:
                        j = n // LAST_PART
                        if layer == 1 and j:
                            copy_out(j - 1)
                        copy_tail(g2 + j, SLOTS * t2 + n + 1, 4 * (j % 2))
                        if layer == 0:
                            act.wait_ge(x_added, X_LAST[0] + j + 1)
                            square_x(j, DG + j)
                            write_h_hi(range(4 * j, 4 * j + 4), KC)
                if layer == 0:
                    def finish(j):
                        act.wait_ge(x_added, X_POOL + j + 1)
                        write_h_hi(range(4 * j, 4 * j + 4), 3 * KC)
                        square_x(j, 2 * DG + j)

                    for j in range(DG):
                        split_hi(TURN_POOL + 1, j)
                        copy_tail(GROUP_POOL + j, SLOTS * TURN_POOL + j + 1, 4 * (j % 2))
                        if j:
                            finish(j - 1)
                    finish(DG - 1)
            copy_out(DG - 1)

        @block.vector
        def _(dve):
            def split_lo(turn, slot):
                dve.wait_ge(hi_split, SLOTS * turn + (slot + 1))
                nc.vector.tensor_tensor(w_lo[:, slot], raw[:, slot], w_hi[:, slot].bitcast(F32), ALU.subtract).then_inc(lo_split, 1)

            def write_h_lo(j, gain_at, n):
                dve.wait_ge(h_hi_ready, n + 1)
                for k in range(4 * j, 4 * j + 4):
                    last = nc.vector.scalar_tensor_tensor(h_hl[:, k, T:2 * T], x_t[:, k, :], gains[:, gain_at + k:gain_at + k + 1],
                                                          h_hl[:, k, 0:T].bitcast(F32), ALU.mult, ALU.subtract)
                last.then_inc(h_ready, 1)

            def mean_rsqrt(total, count, v, r, done, at):
                n = [0]

                def then(ins):
                    n[0] += 1
                    ins.then_inc(done, 1)
                    dve.wait_ge(done, at + n[0])

                mean, t = v
                then(nc.vector.tensor_scalar(mean, total, 1.0 / count, EPS, ALU.mult, ALU.add))
                then(nc.vector.tensor_scalar(t.bitcast(I32), mean.bitcast(I32), 1, None, ALU.arith_shift_right))
                then(nc.vector.tensor_scalar(r.bitcast(I32), t.bitcast(I32), -1.0, float(RSQRT_SEED), ALU.mult, ALU.add))
                for _ in range(3):
                    then(nc.vector.scalar_tensor_tensor(t, r, -0.5, r, ALU.mult, ALU.mult))
                    then(nc.vector.tensor_tensor(t, t, mean, ALU.mult))
                    then(nc.vector.scalar_tensor_tensor(r, t, 1.5, r, ALU.add, ALU.mult))
                assert n[0] == RSQRT_STEPS

            nc.vector.memset(bias_rows[0:NH, :], MASKED).then_inc(bias_filled, 1)
            dve.wait_ge(table_landed, 32)
            nc.vector.transpose(table_t[0:NB, :], table[0:NH, :]).then_inc(table_turned, 1)
            dve.wait_ge(table_turned, 1)
            nc.vector.tensor_copy(table_p[0:NB, :].rearrange("b (q i o) -> b q i o", i=2, o=2),
                                  table_t[0:NB, :].rearrange("b (q o i) -> b q i o", i=2, o=2)).then_inc(table_turned, 1)
            dve.wait_ge(params_turned, 1)
            nc.vector.tensor_copy(gains[:], ps[:, 0, 0:5 * KC])
            nc.vector.tensor_copy(taps_early[:, 0].rearrange("p k c -> p (k c)"), ps[:, 0, 5 * KC:5 * KC + 8 * FC]).then_inc(params_ready, 1)
            dve.wait_ge(params_turned, 2)
            nc.vector.tensor_copy(taps_early[:, 1].rearrange("p k c -> p (k c)"), ps[:, 1, 0:8 * FC]).then_inc(params_ready, 1)
            dve.wait_ge(bias_filled, 1)
            nc.vector.tensor_copy(bias_rows[0:NH, P:2 * P], ps[0:NH, 1, 8 * FC:8 * FC + P]).then_inc(bias_built, 1)

            def copy_x(j):
                for i in (2 * j, 2 * j + 1):
                    dve.wait_ge(x_turned, i + 1)
                    nc.vector.tensor_copy(x_t[:, 2 * i:2 * i + 2, :].rearrange("p c t -> p (c t)"), ps[:, (2 + i) % 8, :]).then_inc(x_copied, 1)

            copy_x(0)
            for j in range(DG):
                if j + 1 < DG:
                    copy_x(j + 1)
                write_h_lo(j, 0, j)
                split_lo(TURN_KV, j)
            dve.wait_ge(cols_landed, 16 * 5)
            nc.vector.tensor_scalar(q_gain_col[:], q_gain_col[:], DH ** -0.5, None, ALU.mult)
            nc.vector.tensor_scalar(neg_sink[:], sink[:], -1.0, None, ALU.mult).then_inc(sink_ready, 1)
            dve.wait_ge(ssq_done, TT)
            mean_rsqrt(token_ssq[:], D, (token_mean[:, 0], token_mean[:, 1]), token_rstd[:], rstd_ready, 0)
            for s in range(SLOTS):
                split_lo(TURN_Q0, s)

            for tt in range(TT):
                dve.wait_ge(kv_squared, tt + 1)
                nc.vector.tensor_reduce(head_ssq[:, tt, 0:NKV], probs[:, tt, :].rearrange("p (h d) -> p h d", h=NKV), AX.X, ALU.add).then_inc(kv_summed, 1)
            dve.wait_ge(kv_summed, TT)
            mean_rsqrt(head_ssq[:, :, 0:NKV], DH, (head_mean[:, 0, :, 0:NKV], head_mean[:, 1, :, 0:NKV]), head_rinv[:, :, 0:NKV], kv_rinv, 0)
            for tt in range(TT):
                rows = q_rows[:, tt, :].rearrange("p (h r d) -> p r h d", h=NKV, r=2)
                for r in range(2):
                    last = nc.vector.scalar_tensor_tensor(
                        rows[:, r], ps[:, 2 + tt, 0:NKV * DH].rearrange("p (h d) -> p h d", h=NKV), token_rstd[:, tt:tt + 1],
                        head_rinv[:, tt, 0:NKV].unsqueeze(2).broadcast_to([P, NKV, DH]), ALU.mult, ALU.mult)
                last.then_inc(k_rows_ready, 1)

            def norm_q(g):
                for tt in range(TT):
                    dve.wait_ge(q_squared, 2 * g + (tt + 1))
                    nc.vector.tensor_reduce(head_ssq[:, tt, :], q_rows[:, tt, :].rearrange("p (h d) -> p h d", h=8), AX.X, ALU.add).then_inc(q_summed, 1)
                dve.wait_ge(q_summed, 2 * g + 2)
                mean_rsqrt(head_ssq[:], DH, (head_mean[:, 0], head_mean[:, 1]), head_rinv[:], q_rinv, g * RSQRT_STEPS)
                for tt in range(TT):
                    nc.vector.scalar_tensor_tensor(
                        q_rows[:, tt, :].rearrange("p (h d) -> p h d", h=8), ps[:, tt, :].rearrange("p (h d) -> p h d", h=8),
                        token_rstd[:, tt:tt + 1], head_rinv[:, tt, :].unsqueeze(2).broadcast_to([P, 8, DH]), ALU.mult, ALU.mult).then_inc(q_ready, 1)

            for s in range(SLOTS):
                split_lo(TURN_Q0 + 1, s)
            norm_q(0)

            def attend(g, turn, last):
                nc.vector.tensor_copy(v_group[:], v_rows[:, :, ds(g, 1) if not last else slice(g, g + 1), :]).then_inc(v_group_ready, 1)

                def bias_and_max(s):
                    half, tt = divmod(s, 2)
                    b, lo = s % 2, P * (1 - tt)
                    heads = (lambda t: t[:, ds(8 * g + 4 * half, 4)] if not last else t[:, 8 * g + 4 * half:8 * g + 4 * half + 4])
                    by_bank = (lambda t: t.rearrange("p (i o) -> p i o", i=2))
                    dve.wait_ge(scores_done, 4 * g + (s + 1))
                    dve.wait_ge(bias_landed[half], 16 * g + 16)
                    dve.wait_ge(probs_turned, 4 * g + s)
                    nc.vector.tensor_tensor(probs[:, :, lo:], ps[:, 2:4, :].rearrange("p b (o k) -> p (b o) k", o=2)[:, :, lo:],
                                            bias_ab[half][:, :, lo:], ALU.add).then_inc(biased, 1)
                    dve.wait_ge(biased, 4 * g + (s + 1))
                    nc.vector.tensor_reduce(row_max[:, b, :], probs[:, :, lo:], AX.X, ALU.max).then_inc(maxed, 1)
                    dve.wait_ge(maxed, 4 * g + (s + 1))
                    nc.vector.scalar_tensor_tensor(by_bank(neg_max[:, b, :]), by_bank(row_max[:, b, :]), -1.0,
                                                   heads(neg_sink).rearrange("p (o i) -> p i o", i=2), ALU.mult, ALU.min).then_inc(neg_max_ready, 1)
                    dve.wait_ge(neg_max_ready, 4 * g + (s + 1))
                    nc.vector.tensor_tensor(by_bank(sink_arg[:, b, :]), by_bank(neg_max[:, b, :]),
                                            heads(sink).rearrange("p (o i) -> p i o", i=2), ALU.add).then_inc(sink_arg_ready, 1)

                def denominators(s):
                    b = s % 2
                    dve.wait_ge(exp_done, 4 * g + (s + 1))
                    nc.vector.tensor_tensor(row_den[:, b, :], row_sum[:, b, :], sink_exp[:, b, :], ALU.add).then_inc(den_ready, 1)
                    dve.wait_ge(den_ready, 4 * g + (s + 1))
                    nc.vector.reciprocal(row_rinv[:, b, :], row_den[:, b, :]).then_inc(rinv_ready, 1)

                def normalise_out(s):
                    b = s % 2
                    dve.wait_ge(pv_done, 4 * g + (s + 1))
                    dve.wait_ge(rinv_ready, 4 * g + (s + 1))
                    nc.vector.tensor_tensor(o_rows[:].rearrange("p (o i) d -> p o i d", i=2),
                                            ps[:, 6, 0:4 * DH].rearrange("p (o i d) -> p o i d", o=2, i=2),
                                            row_rinv[:, b, :].rearrange("p (i o) -> p o i", i=2).unsqueeze(3).broadcast_to([P, 2, 2, DH]),
                                            ALU.mult).then_inc(o_ready, 1)

                def out_lo(s):
                    half, tt = divmod(s, 2)
                    c0 = 4 * g + 2 * half
                    chunks = ds(c0, 2) if not last else slice(c0, c0 + 2)
                    dve.wait_ge(o_hi, 4 * g + (s + 1))
                    nc.vector.tensor_tensor(g_hl[:, chunks, T + tt * P:T + (tt + 1) * P], ps[:, 7, 0:2 * P].rearrange("p (c q) -> p c q", c=2),
                                            g_hl[:, chunks, tt * P:(tt + 1) * P].bitcast(F32), ALU.subtract).then_inc(o_lo, 1)

                bias_and_max(0)
                denominators(0)
                for s in range(4):
                    if s:
                        out_lo(s - 1)
                    if s % 2:
                        dve.wait_ge(probs_turned, 4 * g + (s + 1))
                        nc.vector.tensor_copy(probs_t[:, 1], ps[:, 5, :].rearrange("p (h q) -> p h q", h=4)).then_inc(probs_t_dve, 1)
                    if s < 3:
                        bias_and_max(s + 1)
                    normalise_out(s)
                    if s < 3:
                        split_lo(turn + 1, s)
                        denominators(s + 1)
                if not last:
                    norm_q(g + 1)
                out_lo(3)
                split_lo(turn + 1, 3)

            dve.wait_ge(sink_ready, 1)
            with dve.Fori(0, NKV - 1) as g:
                attend(g, TURN_Q0 + 1 + g, False)
            attend(NKV - 1, TURN_WO, True)

            def sum_squares(n):
                dve.wait_ge(squared, n + 1)
                if n % DG == 0 and n:
                    dve.wait_ge(ssq_all_ready, n // DG)
                nc.vector.tensor_reduce((ssq_part if n % DG else ssq_local)[:], squares[:].rearrange("p c t -> p t c"), AX.X, ALU.add).then_inc(ssq_reduced, 1)
                if n % DG:
                    dve.wait_ge(ssq_reduced, n + 1)
                    nc.vector.tensor_tensor(ssq_local[:], ssq_local[:], ssq_part[:], ALU.add).then_inc(ssq_local_ready, 1)

            def token_rsqrt(n):
                dve.wait_ge(ssq_all_ready, n + 1)
                mean_rsqrt(ssq_all[:], D, (ssq_mean[:, 0], ssq_mean[:, 1]), rstd[:], token_scale, n * RSQRT_STEPS)

            for j in range(DG):
                if j:
                    for s in range(SLOTS):
                        split_lo(TURN_WO + j + 1, s)
                dve.wait_ge(units_done, SLOTS * (TURN_WO + j + 1))
                x_group = x_t[:, 4 * j:4 * j + 4, :].rearrange("p c t -> p (c t)")
                nc.vector.tensor_tensor(x_group, x_group, ps[:, 2 * j:2 * j + 2, :].rearrange("p b n -> p (b n)"), ALU.add).then_inc(banks_added, 1)
                dve.wait_ge(banks_added, j + 1)
                sum_squares(j)
                write_h_lo(j, 2 * KC, DG + j)
            token_rsqrt(0)
            dve.wait_ge(taps_landed, 16)

            def add_banks(group, banks):
                dve.wait_ge(tail_copied, group + (1 - DG))
                nc.vector.tensor_tensor(pre[:], ps[:, banks:banks + 4, 0:T], tail[:], ALU.add).then_inc(banks_added, 1)
                dve.wait_ge(banks_added, group + 1)

            def conv(layer, group, banks, n, y, chunk0):
                add_banks(group, banks)
                nc.vector.tensor_tensor(pre[:], pre[:], rstd[:].unsqueeze(1).broadcast_to([P, 4, T]), ALU.mult).then_inc(pre_scaled, 1)
                dve.wait_ge(pre_scaled, n + 1)

                def tap(k, c):
                    return taps[:, layer, k, ds(chunk0 + c, 1)]

                for c in range(4):
                    last = nc.vector.tensor_scalar(y[:, c, :], pre[:, c, :], tap(2, c), tap(3, c), ALU.mult, ALU.add)
                last.then_inc(tap_mid, 1)
                dve.wait_ge(tap_mid, n + 1)
                for c in range(4):
                    last = nc.vector.scalar_tensor_tensor(y[:, c, 1:T], pre[:, c, 0:T - 1], tap(1, c), y[:, c, 1:T], ALU.mult, ALU.add)
                last.then_inc(tap_prev, 1)
                dve.wait_ge(tap_prev, n + 1)
                for c in range(4):
                    last = nc.vector.scalar_tensor_tensor(y[:, c, 2:T], pre[:, c, 0:T - 2], tap(0, c), y[:, c, 2:T], ALU.mult, ALU.add)
                last.then_inc(conv_done, 1)

            def mlp_group(layer, turn, group, it, i, chunk0):
                for s in range(SLOTS):
                    split_lo(turn + 1, s)
                conv(layer, group, 0, 2 * it, y_gate, chunk0)
                for s in range(SLOTS):
                    split_lo(turn + 2, s)
                conv(layer, group + 1, 4, 2 * it + 1, y_val, chunk0 + FC)
                dve.wait_ge(conv_done, 2 * it + 2)
                dve.wait_ge(silu_done, it + 1)
                nc.vector.tensor_tensor(y_val[:], y_val[:], y_gate[:], ALU.mult).then_inc(gated, 1)
                dve.wait_ge(g_hi, it + 1)
                nc.vector.tensor_tensor(g_hl[:, ds(i * 4, 4), T:2 * T], y_val[:], g_hl[:, ds(i * 4, 4), 0:T].bitcast(F32), ALU.subtract).then_inc(g_lo, 1)

            for layer in range(2):
                t0, g0, it0 = TURN_FFN[layer], GROUP_FFN[layer], ITER_FFN[layer]
                with dve.Fori(0, WHOLE_PARTS) as part:
                    with dve.Fori(0, PART) as i:
                        mlp_group(layer, part * PART_TURNS + i * 2 + t0, part * PART_GROUPS + i * 2 + g0, part * PART + i + it0, i, part * KC + i * 4)
                    with dve.Fori(0, DG // 2) as j2:
                        for b in range(2):
                            turn = part * PART_TURNS + j2 * 2 + (t0 + 2 * PART + b)
                            for s in range(SLOTS):
                                split_lo(turn + 1, s)
                            add_banks(part * PART_GROUPS + j2 * 2 + (g0 + 2 * PART + b), 4 * b)
                            x_group = x_t[:, ds(j2 * 8 + 4 * b, 4), :]
                            nc.vector.tensor_tensor(x_group, x_group, pre[:], ALU.add).then_inc(x_added, 1)
                            dve.wait_ge(x_added, part * DG + j2 * 2 + (X_FFN[layer] + b + 1))
                t1, g1 = t0 + WHOLE_PARTS * PART_TURNS, g0 + WHOLE_PARTS * PART_GROUPS
                with dve.Fori(0, LAST_PART) as i:
                    mlp_group(layer, i * 2 + t1, i * 2 + g1, i + (it0 + WHOLE_PARTS * PART), i, i * 4 + WHOLE_PARTS * KC)
                t2, g2 = t1 + 2 * LAST_PART, g1 + 2 * LAST_PART
                for n in range(DG * LAST_PART):
                    if t2 + 1 + n // SLOTS < TURNS:
                        split_lo(t2 + 1 + n // SLOTS, n % SLOTS)
                    if n % LAST_PART == LAST_PART - 1:
                        j = n // LAST_PART
                        add_banks(g2 + j, 4 * (j % 2))
                        x_group = x_t[:, 4 * j:4 * j + 4, :]
                        nc.vector.tensor_tensor(x_group, x_group, pre[:], ALU.add).then_inc(x_added, 1)
                        dve.wait_ge(x_added, X_LAST[layer] + j + 1)
                        if layer == 0:
                            sum_squares(DG + j)
                            write_h_lo(j, KC, 2 * DG + j)
                if layer == 1:
                    continue
                token_rsqrt(1)
                dve.wait_ge(pool_inv_landed, 16)
                steps = 0
                for j, window in enumerate(POOL_WINDOWS):
                    split_lo(TURN_POOL + 1, j)
                    add_banks(GROUP_POOL + j, 4 * (j % 2))
                    nc.vector.tensor_tensor(pre[:], pre[:], rstd[:].unsqueeze(1).broadcast_to([P, 4, T]), ALU.mult).then_inc(pool_chain, 1)
                    steps += 1
                    dve.wait_ge(pool_chain, steps)
                    src, dst, spare = pre, y_gate, y_val
                    shift = 1
                    while shift < window:
                        nc.vector.tensor_copy(dst[:, :, 0:shift], src[:, :, 0:shift])
                        nc.vector.tensor_tensor(dst[:, :, shift:], src[:, :, shift:], src[:, :, 0:T - shift], ALU.add).then_inc(pool_chain, 1)
                        steps += 1
                        dve.wait_ge(pool_chain, steps)
                        src, dst, spare = dst, spare, dst
                        shift *= 2
                    nc.vector.tensor_tensor(dst[:, :, 0:window - 1], src[:, :, 0:window - 1],
                                            pool_inv[:, j, 0:window - 1].unsqueeze(1).broadcast_to([P, 4, window - 1]), ALU.mult)
                    nc.vector.tensor_scalar(dst[:, :, window - 1:], src[:, :, window - 1:], 1.0 / window, None, ALU.mult).then_inc(pool_chain, 1)
                    steps += 1
                    dve.wait_ge(pool_chain, steps)
                    nc.vector.tensor_tensor(pre[:], dst[:], pre[:], ALU.subtract).then_inc(pool_chain, 1)
                    steps += 1
                    dve.wait_ge(pool_chain, steps)
                    for c in range(4):
                        k = 4 * j + c
                        last = nc.vector.scalar_tensor_tensor(x_t[:, k, :], pre[:, c, :], gains[:, 4 * KC + k:4 * KC + k + 1], x_t[:, k, :], ALU.mult, ALU.add)
                    last.then_inc(x_added, 1)
                    dve.wait_ge(x_added, X_POOL + j + 1)
                    write_h_lo(j, 3 * KC, 3 * DG + j)
                    sum_squares(2 * DG + j)
                token_rsqrt(2)

        @block.tensor
        def _(pe):
            pe.wait_ge(ident_ready, 2)
            pe.wait_ge(params_landed, 16 * 6)
            nc.tensor.transpose(ps[:, 0, 0:5 * KC], gain_rows[0:5 * KC, :], ident[0:5 * KC, 0:5 * KC])
            for l in range(2):
                at = 5 * KC if l == 0 else 0
                for k in range(4):
                    last = nc.tensor.transpose(ps[:, l, at + k * 2 * FC:at + (k + 1) * 2 * FC], conv_rows[0:2 * FC, l, k, :],
                                               ident[0:2 * FC, 0:2 * FC])
                if l == 0:
                    last.then_inc(params_turned, 1)
            pe.wait_ge(table_turned, 2)
            nc.tensor.matmul(ps[0:NH, 1, 8 * FC:8 * FC + P], table_p[0:NB, :], onehot[0:NB, :], start=True, stop=True).then_inc(params_turned, 1)
            for i in range(2 * DG):
                pe.wait_ge(x_landed[i // 2], 16)
                if i == 2 * DG - 2:
                    pe.wait_ge(params_ready, 2)
                    pe.wait_ge(bias_built, 1)
                for c in range(2):
                    for tt in range(TT):
                        last = nc.tensor.transpose(ps[:, (2 + i) % 8, c * T + tt * P:c * T + (tt + 1) * P],
                                                   x_rows[:, tt, (2 * i + c) * P:(2 * i + c + 1) * P], ident[:])
                last.then_inc(x_turned, 1)

            def turn_x(j):
                pe.wait_ge(x_added, X_LAST[1] + j + 1)
                for tt in range(TT):
                    for c in range(4):
                        last = nc.tensor.transpose(ps[:, 4 * (j % 2) + tt, c * P:(c + 1) * P], x_t[:, 4 * j + c, tt * P:(tt + 1) * P], ident[:])
                last.then_inc(out_turned, 1)

            def rows_unit(turn, kq, bank0):
                pe.wait_ge(lo_split, SLOTS * turn + (kq + 1))
                for k in range(4):
                    c = 4 * kq + k
                    for tt in range(TT):
                        a_hi, a_lo = h_hl[:, c, tt * P:(tt + 1) * P], h_hl[:, c, T + tt * P:T + (tt + 1) * P]
                        o = ps[:, bank0 + tt, :]
                        nc.tensor.matmul(o, a_hi, w_hi[:, kq, k, :], start=(c == 0), stop=False)
                        nc.tensor.matmul(o, a_hi, w_lo[:, kq, k, :], start=False, stop=False)
                        last = nc.tensor.matmul(o, a_lo, w_hi[:, kq, k, :], start=False, stop=(c == KC - 1))
                last.then_inc(units_done, 1)

            def narrow_unit(turn, kq, bank0):
                pe.wait_ge(lo_split, SLOTS * turn + (kq + 1))
                for k in range(4):
                    for c in range(4):
                        o = ps[:, bank0 + c // 2, (c % 2) * T:(c % 2 + 1) * T]
                        hi, lo = w_hi[:, kq, k, c * P:(c + 1) * P], w_lo[:, kq, k, c * P:(c + 1) * P]
                        first = kq == 0 and k == 0 and c % 2 == 0
                        ended = kq == 3 and k == 3
                        nc.tensor.matmul(o, hi, g_hl[:, 4 * kq + k, 0:T], start=first, stop=False, skip_group_check=True)
                        nc.tensor.matmul(o, hi, g_hl[:, 4 * kq + k, T:2 * T], start=False, stop=False, skip_group_check=True)
                        last = nc.tensor.matmul(o, lo, g_hl[:, 4 * kq + k, 0:T], start=False, stop=ended, skip_group_check=True)
                last.then_inc(units_done, 1)

            def unit(turn, slot, act_hl, chunk0, banks, first, ended):
                pe.wait_ge(lo_split, SLOTS * turn + (slot + 1))
                for k in range(4):
                    for c in range(4):
                        hi, lo = w_hi[:, slot, k, c * P:(c + 1) * P], w_lo[:, slot, k, c * P:(c + 1) * P]
                        both, left = ps[:, banks + c, :], ps[:, banks + c, 0:T]
                        a_both, a_hi = act_hl[:, chunk0 + k, :], act_hl[:, chunk0 + k, 0:T]
                        if ended and k == 3:
                            nc.tensor.matmul(left, lo, a_hi, start=False, stop=False)
                            last = nc.tensor.matmul(both, hi, a_both, start=False, stop=True)
                        else:
                            nc.tensor.matmul(both, hi, a_both, start=(first and k == 0), stop=False)
                            last = nc.tensor.matmul(left, lo, a_hi, start=False, stop=False)
                last.then_inc(units_done, 1)

            for kq in range(4):
                pe.wait_ge(h_ready, kq + 1)
                rows_unit(TURN_KV, kq, 2)
            for kq in range(4):
                rows_unit(TURN_Q0, kq, 0)
            for tt in range(TT):
                pe.wait_ge(k_rows_ready, tt + 1)
                for h in range(NKV):
                    last = nc.tensor.transpose(ps[:, 4 + tt, h * P:(h + 1) * P], q_rows[:, tt, h * P:(h + 1) * P], ident[:])
                last.then_inc(k_turned, 1)

            def attend(g, turn, run_unit, last_group):
                for tt in range(TT):
                    pe.wait_ge(q_ready, 2 * g + (tt + 1))
                    if tt == 0:
                        pe.wait_ge(o_lo, 4 * g)
                    else:
                        pe.wait_ge(q_t_ready, 2 * g + 1)
                    for c in range(4):
                        last = nc.tensor.matmul(ps[:, 7, c * P:(c + 1) * P], q_rows[:, tt, c * P:(c + 1) * P], mirror[:], start=True, stop=True)
                    last.then_inc(q_turned, 1)

                def scores(s):
                    half, tt = divmod(s, 2)
                    pe.wait_ge(k_group_ready, g + 1)
                    pe.wait_ge(q_t_ready, 2 * g + (tt + 1))
                    pe.wait_ge(biased, 4 * g + s)
                    for a in range(4):
                        r, i, o = DH * (a % 2), a % 2, a // 2
                        out_cols = slice(2 * P * o + P * (1 - tt), 2 * P * (o + 1))
                        last = nc.tensor.matmul(ps[:, 2 + i, out_cols], q_t[r:r + DH, 2 * half + o, tt * P:(tt + 1) * P],
                                                k_group[r:r + DH, 0, 0:P * (tt + 1)], start=True, stop=True)
                    last.then_inc(scores_done, 1)

                def turn_probs(s):
                    pe.wait_ge(exp_done, 4 * g + (s + 1))
                    pe.wait_ge(probs_t_act, 4 * g + s)
                    pe.wait_ge(probs_t_dve, 2 * g + s // 2)
                    for kb in range(1 - s % 2, 2):
                        for j in range(4):
                            last = nc.tensor.transpose(ps[:, 4 + kb, j * P:(j + 1) * P], probs[:, j, kb * P:(kb + 1) * P], ident[:])
                    last.then_inc(probs_turned, 1)

                def values(s):
                    tt = s % 2
                    pe.wait_ge(v_group_ready, g + 1)
                    pe.wait_ge(probs_t_act, 4 * g + (s + 1))
                    pe.wait_ge(probs_t_dve, 2 * g + (s + 1) // 2)
                    pe.wait_ge(o_ready, 4 * g + s)
                    for a in range(4):
                        j = (a % 2) * 2 + a // 2
                        for kb in range(1 - tt, 2):
                            last = nc.tensor.matmul(ps[:, 6, a * DH:(a + 1) * DH], probs_t[:, kb, j, :],
                                                    v_group[:, kb if tt else 0, 0, :], start=(kb == 1 - tt), stop=(kb == 1))
                    last.then_inc(pv_done, 1)

                def turn_out(s):
                    pe.wait_ge(o_ready, 4 * g + (s + 1))
                    pe.wait_ge(o_lo, 4 * g + s)
                    for c in range(2):
                        last = nc.tensor.matmul(ps[:, 7, c * P:(c + 1) * P],
                                                o_rows[:, 2 * c:2 * c + 2, :].rearrange("p a d -> p (a d)"), mirror[:], start=True, stop=True)
                    last.then_inc(o_turned, 1)

                scores(0)
                for s in range(4):
                    if s < 3 or not last_group:
                        run_unit(turn, s)
                    if s:
                        turn_out(s - 1)
                    turn_probs(s)
                    if s < 3:
                        scores(s + 1)
                    values(s)
                turn_out(3)
                if last_group:
                    pe.wait_ge(o_lo, 4 * NKV)
                    run_unit(turn, 3)

            def q_unit(turn, kq):
                if kq == 0:
                    pe.wait_ge(q_ready, 2 * turn - 2 * TURN_Q0)
                rows_unit(turn, kq, 0)

            with pe.Fori(0, NKV - 1) as g:
                attend(g, TURN_Q0 + 1 + g, q_unit, False)
            attend(NKV - 1, TURN_WO, lambda turn, kq: narrow_unit(turn, kq, 0), True)
            for j in range(1, DG):
                for kq in range(4):
                    narrow_unit(TURN_WO + j, kq, 2 * j)

            def mlp_group(turn, group, h_steps):
                for half in range(2):
                    pe.wait_ge(banks_added, group + (half - 1))
                    for kq in range(4):
                        pe.wait_ge(h_ready, h_steps + kq + 1)
                        unit(turn + half, kq, h_hl, 4 * kq, 4 * half, kq == 0, kq == 3)

            for layer in range(2):
                t0, g0, it0 = TURN_FFN[layer], GROUP_FFN[layer], ITER_FFN[layer]
                h_steps = DG if layer == 0 else 3 * DG
                with pe.Fori(0, WHOLE_PARTS) as part:
                    with pe.Fori(0, PART) as i:
                        mlp_group(part * PART_TURNS + i * 2 + t0, part * PART_GROUPS + i * 2 + g0, h_steps)
                    with pe.Fori(0, DG // 2) as j2:
                        for b in range(2):
                            pe.wait_ge(banks_added, part * PART_GROUPS + j2 * 2 + (g0 + 2 * PART + b - 1))
                            for kq in range(PART):
                                pe.wait_ge(g_lo, part * PART + (it0 + kq + 1))
                                unit(part * PART_TURNS + j2 * 2 + (t0 + 2 * PART + b), kq, g_hl, 4 * kq, 4 * b, kq == 0, kq == PART - 1)
                t1, g1 = t0 + WHOLE_PARTS * PART_TURNS, g0 + WHOLE_PARTS * PART_GROUPS
                with pe.Fori(0, LAST_PART) as i:
                    mlp_group(i * 2 + t1, i * 2 + g1, h_steps)
                t2, g2 = t1 + 2 * LAST_PART, g1 + 2 * LAST_PART
                for n in range(DG * LAST_PART):
                    j, kq = divmod(n, LAST_PART)
                    if kq == 0:
                        pe.wait_ge(banks_added, g2 + j - 1)
                        if layer == 1 and j >= 2:
                            pe.wait_ge(out_copied, j - 1)
                    pe.wait_ge(g_lo, it0 + WHOLE_PARTS * PART + kq + 1)
                    unit(t2 + n // SLOTS, n % SLOTS, g_hl, 4 * kq, 4 * (j % 2), kq == 0, kq == LAST_PART - 1)
                    if layer == 1 and kq == LAST_PART - 2 and j:
                        turn_x(j - 1)
                if layer == 0:
                    for j in range(DG):
                        pe.wait_ge(banks_added, GROUP_POOL + j - 1)
                        pe.wait_ge(h_ready, 2 * DG + j + 1)
                        unit(TURN_POOL, j, h_hl, 4 * j, 4 * (j % 2), True, True)
            turn_x(DG - 1)


_INS = ["x", "norm_mix", "norm_ffn", "rel_bias", "attn_w_qkv", "attn_q_gain", "attn_k_gain", "attn_sinks", "attn_w_o",
        "pool_w", "pool_scale", "ffn_w_up", "ffn_conv_w", "ffn_conv_b", "ffn_w_down"]


def _bucket_onehot(n_buckets, window, max_distance=128):
    import numpy as np
    n = np.arange(window)[::-1]
    exact = n_buckets // 2
    nf = np.maximum(n, 1).astype(np.float32)
    large = exact + (np.log(nf / exact) / np.log(max_distance / exact) * (n_buckets - exact)).astype(np.int32)
    bucket = np.where(n < exact, n, np.minimum(large, n_buckets - 1))
    return (np.arange(n_buckets)[:, None] == bucket[None, :]).astype(np.float32)


def _inv_count(windows):
    import numpy as np
    t = np.arange(max(windows))[None, :]
    return (1.0 / np.minimum(t + 1, np.array(windows)[:, None])).astype(np.float32)


def kernel(**inputs):
    import numpy as np
    from concourse import bacc
    from concourse.bass_utils import run_bass_kernel_spmd

    nc = bacc.Bacc("TRN2", target_bir_lowering=False, num_devices=1)
    given = {name: np.ascontiguousarray(inputs[name]) for name in _INS}
    given["bucket_onehot"] = _bucket_onehot(given["rel_bias"].shape[1], 128)
    given["inv_count"] = _inv_count(POOL_WINDOWS)
    arrays, args = {}, []
    for name, a in given.items():
        arrays[f"in_{name}"] = a
        args.append(nc.dram_tensor(f"in_{name}", a.shape, mybir.dt.from_np(a.dtype), kind="ExternalInput").ap())
    out = nc.dram_tensor("out", given["x"].shape, F32, kind="ExternalOutput").ap()
    build_trunk(nc, *args, out)
    return run_bass_kernel_spmd(nc, [arrays], core_ids=[0]).results[0]["out"]
```

```python
from contextlib import ExitStack

import concourse.bass as bass
from concourse import mybir

F32 = mybir.dt.float32
F32R = mybir.dt.float32r
I32 = mybir.dt.int32
ALU = mybir.AluOpType
ACT = mybir.ActivationFunctionType
AX = mybir.AxisListType
ds = bass.ds

P = 128
SLOTS = 4
UNIT_K = 4
UNIT_N = 512
POOL_WINDOWS = (2, 4, 8, 16)
EPS = 1e-6
RSQRT_SEED = 0x5F3759DF
RSQRT_STEPS = 12
MASKED = -1e30
MAP_REACH = max(POOL_WINDOWS)
MAP_COLS = 2 * P + MAP_REACH
BIAS_ROW = 3 * P


def build_trunk(nc, x_in, norm_mix, norm_ffn, rel_bias, w_qkv, q_gain, k_gain, sinks, w_o, w_pool,
                pool_scale, w_up, conv_w, conv_b, w_down, bucket_onehot, pool_maps, out):
    T, D = x_in.shape[1], x_in.shape[2]
    DH = q_gain.shape[1]
    NH = sinks.shape[1]
    NB = rel_bias.shape[1]
    NKV = (w_qkv.shape[2] // DH - NH) // 2
    F = w_down.shape[1]
    KC = D // P
    FC = F // P
    TT = T // P
    DG = D // UNIT_N
    FG = F // UNIT_N
    PART = KC // UNIT_K
    WHOLE_PARTS = FG // PART
    LAST_PART = FG - WHOLE_PARTS * PART
    assert (T, TT, DG, NKV, KC, LAST_PART) == (256, 2, 4, 4, 16, 3) and NH == 8 * NKV and NH == NB == 32 and 2 * DH == P

    TURN_KV, TURN_Q0, TURN_WO = 0, 1, 1 + NKV
    TURN_FFN = [TURN_WO + DG, 0]
    PART_TURNS = 2 * PART + DG
    FFN_TURNS = WHOLE_PARTS * PART_TURNS + 2 * LAST_PART + DG * LAST_PART // UNIT_K
    TURN_POOL = TURN_FFN[0] + FFN_TURNS
    TURN_FFN[1] = TURN_POOL + 1
    TURNS = TURN_FFN[1] + FFN_TURNS
    PART_GROUPS = 2 * PART + DG
    FFN_GROUPS = WHOLE_PARTS * PART_GROUPS + 2 * LAST_PART + DG
    GROUP_FFN = [DG, DG + FFN_GROUPS]
    ITER_FFN = [0, FG]
    X_FFN = [0, (WHOLE_PARTS + 2) * DG - 1]
    X_LAST = [n + WHOLE_PARTS * DG for n in X_FFN]
    X_POOL = (WHOLE_PARTS + 1) * DG - 1
    X_BANKS = [1, 4, 5, 6, 7, 1, 4, 5]
    OUT_BANKS = [6, 4, 0, 2]
    STEP_CHUNKS = [0, 7, 10, 13, KC]
    LAST_STEP_CHUNKS = [0, 6, 8, 10, KC - 4]
    PARTS = [PART] * WHOLE_PARTS + [LAST_PART]
    FIRST_UNITS = [(half, kq) for kq in range(UNIT_K) for half in range(2)]
    LAST_UNITS = [(j, kq) for kq in range(LAST_PART) for j in range(2)] + [(j, kq) for j in range(2, DG) for kq in range(LAST_PART)]

    def first_in_loop(layer, part):
        return 2 if (layer, part) == (1, 0) else 0

    def part_start(layer, part):
        return TURN_FFN[layer] + part * PART_TURNS, GROUP_FFN[layer] + part * PART_GROUPS, ITER_FFN[layer] + part * PART

    qkv_v = w_qkv[0].rearrange("(k p) n -> p k n", p=P)
    wo_v = w_o[0].rearrange("(k p) n -> p k n", p=P)
    up_v = [w_up[l].rearrange("(k p) n -> p k n", p=P) for l in range(2)]
    down_v = [w_down[l].rearrange("(k p) n -> p k n", p=P) for l in range(2)]
    pool_v = [w_pool[0, g].rearrange("(k p) n -> p k n", p=P) for g in range(DG)]
    x_v = x_in[0].rearrange("(t p) d -> p t d", p=P)
    out_v = out[0].rearrange("(t p) d -> p t d", p=P)
    bias_rows_dram = nc.dram_tensor("bias_rows_dram", [NH, BIAS_ROW], F32)
    taps_dram = nc.dram_tensor("taps_dram", [P, 2 * 4 * 2 * FC], F32)

    place_at = [(nc.sbuf_base + 31) // 32 * 32]

    def place(name, shape, dt=F32):
        n = 4
        for d in shape[1:]:
            n *= d
        t = nc.alloc_sbuf_tensor_at(name, [P] + list(shape[1:]), dt, offset=place_at[0])
        place_at[0] += (n + 31) // 32 * 32
        return t

    x_t = place("x_t", [P, KC, T])
    h_hl = place("h_hl", [P, KC, 2 * T], F32R)
    g_at = place_at[0]
    g_hl = place("g_hl", [P, KC, 2 * T], F32R)
    raw = place("raw", [P, SLOTS, UNIT_K, UNIT_N])
    w_hi = place("w_hi", [P, SLOTS, UNIT_K, UNIT_N], F32R)
    w_lo = place("w_lo", [P, SLOTS, UNIT_K, UNIT_N], F32R)
    ident = place("ident", [P, P])
    mirror = place("mirror", [P, P])
    ones = place("ones", [P, 1])
    gains = place("gains", [P, 5 * KC])
    token_ssq = place("token_ssq", [P, TT])
    token_mean = place("token_mean", [P, 2, TT])
    token_rstd = place("token_rstd", [P, TT])
    q_gain_col = place("q_gain_col", [P, 1])
    k_gain_col = place("k_gain_col", [P, 1])
    neg_sink = place("neg_sink", [P, NH])
    sink = place("sink", [P, NH])
    stage_at = place_at[0]
    x_rows = place("x_rows", [P, TT, D])
    conv_rows = place("conv_rows", [P, 2, 4, P])
    gain_rows = place("gain_rows", [P, P])
    table = place("table", [P, NB])
    table_t = place("table_t", [P, NH])
    table_p = place("table_p", [P, NH])
    onehot = place("onehot", [P, P])
    bias_rows = place("bias_rows", [P, BIAS_ROW])
    taps_early = place("taps_early", [P, 2, 4, 2 * FC])
    place_at[0] = stage_at
    probs = place("probs", [P, 4, 2 * P])
    probs_t = place("probs_t", [P, 2, 4, P])
    q_rows = place("q_rows", [P, TT, UNIT_N])
    q_t = place("q_t", [P, 4, T])
    k_t = place("k_t", [P, NKV, T])
    k_group = place("k_group", [P, 1, T])
    v_rows = place("v_rows", [P, TT, NKV, DH])
    v_group = place("v_group", [P, TT, 1, DH])
    o_rows = place("o_rows", [P, 4, DH])
    bias_b = place("bias_b", [P, 4, 2 * P])
    head_ssq = place("head_ssq", [P, TT, 8])
    head_mean = place("head_mean", [P, 2, TT, 8])
    head_rinv = place("head_rinv", [P, TT, 8])
    row_max = place("row_max", [P, 2, 4])
    neg_max = place("neg_max", [P, 2, 4])
    row_sum = place("row_sum", [P, 2, 4])
    sink_arg = place("sink_arg", [P, 2, 4])
    sink_exp = place("sink_exp", [P, 2, 4])
    row_den = place("row_den", [P, 2, 4])
    row_rinv = place("row_rinv", [P, 2, 4])
    assert place_at[0] <= nc.sbuf_usable_end, (place_at[0], nc.sbuf_usable_end)
    bias_a = nc.alloc_sbuf_tensor_at("bias_a", [P, 4, 2 * P], F32, offset=g_at + (KC - 2) * 2 * T * 4)
    bias_ab = [bias_a, bias_b]
    q_squares = nc.alloc_sbuf_tensor_at("q_squares", [P, TT, UNIT_N], F32, offset=g_at + (KC - 4) * 2 * T * 4)
    z_rows = nc.alloc_sbuf_tensor_at("z_rows", [P, TT, D], F32, offset=g_at)
    pool_map = nc.alloc_sbuf_tensor_at("pool_map", [P, DG, MAP_COLS], F32, offset=g_at + LAST_PART * UNIT_K * 2 * T * 4)
    place_at[0] = stage_at
    tail = place("tail", [P, 4, T])
    pre = place("pre", [P, 4, T])
    y_gate = place("y_gate", [P, 4, T])
    y_val = place("y_val", [P, 4, T])
    squares = place("squares", [P, 4, T])
    ssq_part = place("ssq_part", [P, T])
    ssq_local = place("ssq_local", [P, T])
    ssq_all = place("ssq_all", [P, T])
    ssq_mean = place("ssq_mean", [P, 2, T])
    rstd = place("rstd", [P, T])
    taps = place("taps", [P, 2, 4, 2 * FC])
    assert place_at[0] <= nc.sbuf_usable_end


    def squares_for(n):
        return y_val if n > 2 * DG and n % 2 else squares

    with ExitStack() as ctx:
        ps = ctx.enter_context(nc.psum_tensor("ps", [P, 8, UNIT_N], F32))

        def sem(name):
            return ctx.enter_context(nc.semaphore(name))

        raw_landed = [sem(f"raw_landed{s}") for s in range(SLOTS)]
        hi_split, lo_split, units_done = sem("hi_split"), sem("lo_split"), sem("units_done")
        x_landed = [sem(f"x_landed{i}") for i in range(4)]
        params_landed, cols_landed, table_landed = sem("params_landed"), sem("cols_landed"), sem("table_landed")
        table_turned = sem("table_turned")
        ident_zero, ident_ready = sem("ident_zero"), sem("ident_ready")
        gains_landed, gains_turned, gains_ready = sem("gains_landed"), sem("gains_turned"), sem("gains_ready")
        params_turned, params_ready = sem("params_turned"), sem("params_ready")
        x_turned, x_copied = sem("x_turned"), sem("x_copied")
        bias_filled, bias_built, bias_stored = sem("bias_filled"), sem("bias_built"), sem("bias_stored")
        bias_landed = [sem("bias_landed_a"), sem("bias_landed_b")]
        ssq_done, rstd_ready, sink_ready = sem("ssq_done"), sem("rstd_ready"), sem("sink_ready")
        h_hi_ready, h_ready = sem("h_hi_ready"), sem("h_ready")
        kv_squared, kv_summed, kv_rinv, k_rows_ready = sem("kv_squared"), sem("kv_summed"), sem("kv_rinv"), sem("k_rows_ready")
        k_turned, k_t_ready = sem("k_turned"), sem("k_t_ready")
        q_copied_act, q_copied_dve = sem("q_copied_act"), sem("q_copied_dve")
        q_squared, q_summed, q_sums_turned, q_rinv = sem("q_squared"), sem("q_summed"), sem("q_sums_turned"), sem("q_rinv")
        q_turned, q_t_act, q_t_dve = sem("q_turned"), sem("q_t_act"), sem("q_t_dve")
        k_group_ready, v_group_ready = sem("k_group_ready"), sem("v_group_ready")
        scores_done, biased, maxed, neg_max_ready = sem("scores_done"), sem("biased"), sem("maxed"), sem("neg_max_ready")
        sink_arg_ready, exp_done, den_ready, rinv_ready = sem("sink_arg_ready"), sem("exp_done"), sem("den_ready"), sem("rinv_ready")
        probs_turned, probs_t_act, probs_t_dve = sem("probs_turned"), sem("probs_t_act"), sem("probs_t_dve")
        pv_done, o_ready, o_turned, o_hi, o_lo = sem("pv_done"), sem("o_ready"), sem("o_turned"), sem("o_hi"), sem("o_lo")
        tail_copied, banks_added = sem("tail_copied"), sem("banks_added")
        x_added = sem("x_added")
        squared, ssq_reduced, ssq_local_ready, ssq_all_ready, token_scale = sem("squared"), sem("ssq_reduced"), sem("ssq_local_ready"), sem("ssq_all_ready"), sem("token_scale")
        pre_scaled, tap_mid, tap_prev, conv_done = sem("pre_scaled"), sem("tap_mid"), sem("tap_prev"), sem("conv_done")
        silu_done, gated, g_hi, g_lo = sem("silu_done"), sem("gated"), sem("g_hi"), sem("g_lo")
        taps_landed = sem("taps_landed")
        pool_map_landed, z_ready, pooled = sem("pool_map_landed"), sem("z_ready"), sem("pooled")
        token_sums_turned, mixer_scale = sem("token_sums_turned"), sem("mixer_scale")
        out_turned, out_copied = sem("out_turned"), sem("out_copied")
        out_stored = [sem("out_stored_even"), sem("out_stored_odd")]

        block = ctx.enter_context(nc.Block())

        @block.sync
        def _(sp):
            sp.dma_start(gain_rows[0:2 * KC, :], norm_mix.rearrange("l (c p) -> (l c) p", p=P)).then_inc(gains_landed, 16)
            sp.dma_start(gain_rows[2 * KC:4 * KC, :], norm_ffn.rearrange("l (c p) -> (l c) p", p=P)).then_inc(gains_landed, 16)
            sp.dma_start(gain_rows[4 * KC:5 * KC, :], pool_scale[0].rearrange("(c p) -> c p", p=P)).then_inc(gains_landed, 16)

            def load(turn, slot, src, first=False):
                if not first:
                    sp.wait_ge(lo_split, SLOTS * turn + (slot + 1 - SLOTS))
                sp.dma_start(raw[:, slot], src).then_inc(raw_landed[slot], 16)

            def load_x(j):
                w = D // 4
                sp.dma_start(x_rows[:, :, j * w:(j + 1) * w], x_v[:, :, j * w:(j + 1) * w]).then_inc(x_landed[j], 16)

            load_x(0)
            for kq in range(4):
                if kq + 1 < 4:
                    load_x(kq + 1)
                load(TURN_KV, kq, qkv_v[:, 4 * kq:4 * kq + 4, D:D + UNIT_N], first=True)
            with sp.Fori(0, NKV) as g:
                for kq in range(4):
                    load(TURN_Q0 + g, kq, qkv_v[:, 4 * kq:4 * kq + 4, ds(g * UNIT_N, UNIT_N)])
            with sp.Fori(0, DG) as j:
                for kq in range(4):
                    load(TURN_WO + j, kq, wo_v[:, 4 * kq:4 * kq + 4, ds(j * UNIT_N, UNIT_N)])

            def load_up(layer, turn, f):
                for half in range(2):
                    for kq in range(4):
                        load(turn + half, kq, up_v[layer][:, 4 * kq:4 * kq + 4, ds(f * UNIT_N + half * F, UNIT_N)])

            for layer in range(2):
                for part, size in enumerate(PARTS):
                    turn = part_start(layer, part)[0]
                    if (layer, part) == (1, 0):
                        for n, (half, kq) in enumerate(FIRST_UNITS):
                            load(turn + n // SLOTS, n % SLOTS, up_v[layer][:, 4 * kq:4 * kq + 4, half * F:half * F + UNIT_N])
                        for half in range(2):
                            for kq in range(4):
                                load(turn + 2 + half, kq, up_v[layer][:, 4 * kq:4 * kq + 4, UNIT_N + half * F:2 * UNIT_N + half * F])
                    with sp.Fori(first_in_loop(layer, part), size) as i:
                        load_up(layer, i * 2 + turn, i + part * PART)
                    if part < WHOLE_PARTS:
                        with sp.Fori(0, DG) as j:
                            for kq in range(4):
                                load(j + (turn + 2 * PART), kq,
                                     down_v[layer][:, part * KC + 4 * kq:part * KC + 4 * kq + 4, ds(j * UNIT_N, UNIT_N)])
                    else:
                        for n, (j, kq) in enumerate(LAST_UNITS):
                            k = part * KC + 4 * kq
                            load(turn + 2 * size + n // SLOTS, n % SLOTS, down_v[layer][:, k:k + 4, j * UNIT_N:(j + 1) * UNIT_N])
                if layer == 0:
                    for g in range(DG):
                        load(TURN_POOL, g, pool_v[g])
            for j in range(DG):
                sp.wait_ge(out_copied, j + 1)
                sp.dma_start(out_v[:, :, j * UNIT_N:(j + 1) * UNIT_N],
                             (y_gate if j % 2 == 0 else y_val)[:].rearrange("p a t -> p (a t)").rearrange(
                                 "p (t d) -> p t d", t=TT)).then_inc(out_stored[j % 2], 16)
            for b in range(2):
                sp.wait_ge(out_stored[b], 16 * (DG // 2))

        @block.gpsimd
        def _(pool):
            nc.gpsimd.memset(ident[:], 0.0).then_inc(ident_zero, 1)
            nc.gpsimd.memset(mirror[:], 0.0).then_inc(ident_zero, 1)
            nc.gpsimd.memset(ones[:], 1.0).then_inc(ident_zero, 1)
            pool.wait_ge(ident_zero, 3)
            nc.gpsimd.affine_select(out=ident[:], in_=ident[:], compare_op=ALU.not_equal, fill=1.0, base=0,
                                    pattern=[[-1, P]], channel_multiplier=1).then_inc(ident_ready, 1)
            nc.gpsimd.affine_select(out=mirror[:], in_=mirror[:], compare_op=ALU.not_equal, fill=1.0, base=1 - P,
                                    pattern=[[1, P]], channel_multiplier=1).then_inc(ident_ready, 1)
            for l in range(2):
                pool.dma_start(conv_rows[0:2 * FC, l, 0:3, :], conv_w[l].rearrange("k (c p) -> c k p", p=P)).then_inc(params_landed, 16)
            pool.dma_start(conv_rows[0:2 * FC, :, 3, :], conv_b.rearrange("l (c p) -> c l p", p=P)).then_inc(params_landed, 16)
            pool.dma_start(table[0:NH, :], rel_bias).then_inc(table_landed, 16)
            pool.dma_start(onehot[0:NB, :], bucket_onehot).then_inc(table_landed, 16)
            for r in range(2):
                pool.dma_start(q_gain_col[r * DH:(r + 1) * DH, :], q_gain.rearrange("a d -> d a"), allow_slow_non_contiguous=True).then_inc(cols_landed, 16)
                pool.dma_start(k_gain_col[r * DH:(r + 1) * DH, :], k_gain.rearrange("a d -> d a"), allow_slow_non_contiguous=True).then_inc(cols_landed, 16)
            pool.dma_start(sink[:], sinks.broadcast_to([P, NH])).then_inc(cols_landed, 16)
            pool.wait_ge(bias_built, 1)
            pool.dma_start(bias_rows_dram.ap()[:, :], bias_rows[0:NH, :]).then_inc(bias_stored, 16)
            pool.wait_ge(params_ready, 2)
            pool.dma_start(taps_dram.ap()[:, :], taps_early[:].rearrange("p l k c -> p (l k c)")).then_inc(bias_stored, 16)
            pool.wait_ge(bias_stored, 32)

            def load_bias(g, half):
                src = bass.AP(tensor=bias_rows_dram, offset=(g * 8 + 4 * half) * BIAS_ROW,
                              ap=[[1, P], [BIAS_ROW, 4], [1, 2 * P]])
                pool.dma_start(bias_ab[half][:], src).then_inc(bias_landed[half], 16)

            for half in range(2):
                if half == 1:
                    pool.wait_ge(k_rows_ready, TT)
                load_bias(0, half)
            with pool.Fori(1, NKV) as g:
                for half in range(2):
                    pool.wait_ge(biased, 4 * g - 2 + 2 * half)
                    load_bias(g, half)
            pool.wait_ge(biased, 4 * NKV)
            pool.wait_ge(banks_added, 1)
            pool.dma_start(taps[:].rearrange("p l k c -> p (l k c)"), taps_dram.ap()[:, :]).then_inc(taps_landed, 16)
            for layer in range(2):
                if layer == 1:
                    pool.wait_ge(units_done, SLOTS * part_start(0, WHOLE_PARTS)[0])
                    pool.dma_start(pool_map[:].rearrange("p g t -> p (g t)"), pool_maps).then_inc(pool_map_landed, 16)
                pool.wait_ge(ssq_local_ready, (DG - 1) * (1 if layer == 0 else 3))
                if layer == 1:
                    pool.wait_ge(token_scale, RSQRT_STEPS)
                nc.gpsimd.partition_all_reduce(ssq_all[:], ssq_local[:], P, bass.bass_isa.ReduceOp.add).then_inc(ssq_all_ready, 1)

        @block.scalar
        def _(act):
            def copy_out(j):
                act.wait_ge(out_turned, j + 1)
                if j >= 2:
                    act.wait_ge(out_stored[j % 2], 16 * (j // 2))
                nc.scalar.copy((y_gate if j % 2 == 0 else y_val)[:].rearrange("p a t -> p (a t)"),
                               ps[:, OUT_BANKS[j]:OUT_BANKS[j] + 2, :].rearrange("p b n -> p (b n)")).then_inc(out_copied, 1)

            def split_hi(turn, slot, first=False):
                act.wait_ge(raw_landed[slot], 16 * (turn + 1))
                if not first:
                    act.wait_ge(units_done, SLOTS * turn + (slot + 1 - SLOTS))
                nc.scalar.copy(w_hi[:, slot], raw[:, slot]).then_inc(hi_split, 1)

            def write_h_hi(chunks, gain_at):
                for k in chunks:
                    last = nc.scalar.activation(h_hl[:, k, 0:T], x_t[:, k, :], ACT.Identity, scale=gains[:, gain_at + k:gain_at + k + 1])
                last.then_inc(h_hi_ready, 1)

            act.wait_ge(gains_ready, 1)
            for j in range(DG):
                act.wait_ge(x_copied, 2 * j + 2)
                write_h_hi(range(4 * j, 4 * j + 4), 0)
                split_hi(TURN_KV, j, first=True)
            for i in range(4):
                act.wait_ge(x_landed[i], 16)
            for tt in range(TT):
                nc.scalar.activation(g_hl[:, 4 * tt:4 * tt + 4, :].rearrange("p c t -> p (c t)"), x_rows[:, tt, :], ACT.Square,
                                     accum_out=token_ssq[:, tt:tt + 1]).then_inc(ssq_done, 1)

            for s in range(SLOTS):
                split_hi(TURN_Q0, s)
            act.wait_ge(rstd_ready, RSQRT_STEPS)
            act.wait_ge(bias_stored, 32)
            act.wait_ge(units_done, SLOTS * TURN_Q0)
            for tt in range(TT):
                nc.scalar.activation(v_rows[:, tt].rearrange("p h d -> p (h d)"), ps[:, 2 + tt, NKV * DH:2 * NKV * DH],
                                     ACT.Identity, scale=token_rstd[:, tt:tt + 1])
                nc.scalar.activation(probs[:, tt, :], ps[:, 2 + tt, 0:NKV * DH], ACT.Square,
                                     scale=token_rstd[:, tt:tt + 1]).then_inc(kv_squared, 1)

            def copy_q(g, turn):
                act.wait_ge(units_done, SLOTS * turn + SLOTS)
                nc.scalar.activation(q_rows[:, 0, :], ps[:, 0, :], ACT.Identity, scale=token_rstd[:, 0:1]).then_inc(q_copied_act, 1)

            def square_q(g):
                nc.scalar.activation(q_squares[:, 0, :], ps[:, 0, :], ACT.Square, scale=token_rstd[:, 0:1])
                act.wait_ge(q_copied_dve, g + 1)
                nc.scalar.activation(q_squares[:, 1, :], ps[:, 1, :], ACT.Square, scale=token_rstd[:, 1:2]).then_inc(q_squared, 1)

            def turned_q(g, group):
                nc.scalar.copy(k_group[:], k_t[:, group, :]).then_inc(k_group_ready, 1)
                act.wait_ge(q_turned, 2 * g + 1)
                nc.scalar.activation(q_t[:, :, 0:P], ps[:, 2, :].rearrange("p (c q) -> p c q", c=4),
                                     ACT.Identity, scale=q_gain_col[:, 0:1]).then_inc(q_t_act, 1)

            split_hi(TURN_Q0 + 1, 0)
            split_hi(TURN_Q0 + 1, 1)
            act.wait_ge(cols_landed, 16 * 5)
            for tt in range(TT):
                act.wait_ge(k_turned, tt + 1)
                nc.scalar.activation(k_t[:, :, tt * P:(tt + 1) * P], ps[:, 4 + tt, :].rearrange("p (h q) -> p h q", h=NKV),
                                     ACT.Identity, scale=k_gain_col[:, 0:1]).then_inc(k_t_ready, 1)
            split_hi(TURN_Q0 + 1, 2)
            copy_q(0, TURN_Q0)
            square_q(0)
            act.wait_ge(k_t_ready, TT)
            turned_q(0, slice(0, 1))
            split_hi(TURN_Q0 + 1, 3)

            def attend(g, turn, last):
                def exps(s):
                    b, lo = s % 2, P * (1 - s % 2)
                    act.wait_ge(neg_max_ready, 4 * g + (s + 1))
                    for j in range(4):
                        nc.scalar.activation(probs[:, j, lo:], probs[:, j, lo:], ACT.Exp, bias=neg_max[:, b, j:j + 1],
                                             accum_out=row_sum[:, b, j:j + 1])
                    act.wait_ge(sink_arg_ready, 4 * g + (s + 1))
                    nc.scalar.activation(sink_exp[:, b, :], sink_arg[:, b, :], ACT.Exp).then_inc(exp_done, 1)

                def turned_out(s):
                    half, tt = divmod(s, 2)
                    act.wait_ge(o_turned, 4 * g + (s + 1))
                    c0 = 4 * g + 2 * half
                    nc.scalar.copy(g_hl[:, ds(c0, 2) if not last else slice(c0, c0 + 2), tt * P:(tt + 1) * P],
                                   ps[:, 7, 0:2 * P].rearrange("p (c q) -> p c q", c=2)).then_inc(o_hi, 1)

                exps(0)
                for s in range(4):
                    if s == 3 and not last:
                        copy_q(g + 1, turn)
                    if s:
                        turned_out(s - 1)
                    act.wait_ge(probs_turned, 4 * g + (s + 1))
                    kb = 1 - s % 2
                    nc.scalar.copy(probs_t[:, kb], ps[:, 4 + kb, :].rearrange("p (h q) -> p h q", h=4)).then_inc(probs_t_act, 1)
                    if s < 3 and not last:
                        split_hi(turn + 1, s)
                    if s in (1, 2) and last:
                        split_hi(turn + 1, s - 1)
                    if s < 3:
                        exps(s + 1)
                if not last:
                    square_q(g + 1)
                    turned_q(g + 1, ds(g + 1, 1))
                turned_out(3)
                if last:
                    split_hi(turn + 1, 2)
                split_hi(turn + 1, 3)

            with act.Fori(0, NKV - 1) as g:
                attend(g, TURN_Q0 + 1 + g, False)
            attend(NKV - 1, TURN_WO, True)

            def square_x(group, n):
                if 0 < n <= 2 * DG:
                    act.wait_ge(ssq_reduced, n)
                elif n > 2 * DG + 1:
                    act.wait_ge(ssq_reduced, n - 1)
                nc.scalar.activation(squares_for(n)[:], x_t[:, 4 * group:4 * group + 4, :], ACT.Square).then_inc(squared, 1)

            for j in range(DG):
                if j:
                    for s in range(SLOTS):
                        split_hi(TURN_WO + j + 1, s)
                act.wait_ge(banks_added, j + 1)
                square_x(j, j)
                write_h_hi(range(4 * j, 4 * j + 4), 2 * KC)

            def copy_tail(group, end_unit, banks):
                act.wait_ge(units_done, end_unit)
                act.wait_ge(banks_added, group)
                nc.scalar.copy(tail[:], ps[:, banks:banks + 4, T:2 * T]).then_inc(tail_copied, 1)

            def mlp_group(turn, group, it, chunks, split=0):
                for s in range(split, SLOTS):
                    split_hi(turn + 1, s)
                copy_tail(group, SLOTS * turn + SLOTS, 0)
                split_hi(turn + 2, 0)
                split_hi(turn + 2, 1)
                act.wait_ge(conv_done, 2 * it + 1)
                nc.scalar.activation(y_gate[:], y_gate[:], ACT.Silu).then_inc(silu_done, 1)
                split_hi(turn + 2, 2)
                split_hi(turn + 2, 3)
                copy_tail(group + 1, SLOTS * turn + 2 * SLOTS, 4)
                act.wait_ge(gated, it + 1)
                nc.scalar.copy(g_hl[:, chunks, 0:T], y_val[:]).then_inc(g_hi, 1)

            def first_mlp_group(turn, group, it):
                split_hi(turn + 2, 0)
                split_hi(turn + 2, 1)
                copy_tail(group, SLOTS * turn + 2 * SLOTS - 1, 0)
                split_hi(turn + 2, 2)
                split_hi(turn + 2, 3)
                copy_tail(group + 1, SLOTS * turn + 2 * SLOTS, 4)
                act.wait_ge(conv_done, 2 * it + 1)
                nc.scalar.activation(y_gate[:], y_gate[:], ACT.Silu).then_inc(silu_done, 1)
                split_hi(turn + 3, 0)
                split_hi(turn + 3, 1)
                act.wait_ge(gated, it + 1)
                nc.scalar.copy(g_hl[:, 0:4, 0:T], y_val[:]).then_inc(g_hi, 1)

            for layer in range(2):
                for part, size in enumerate(PARTS):
                    turn, group, it = part_start(layer, part)
                    if (layer, part) == (1, 0):
                        first_mlp_group(turn, group, it)
                        mlp_group(turn + 2, group + 2, it + 1, slice(4, 8), split=2)
                    with act.Fori(first_in_loop(layer, part), size) as i:
                        mlp_group(i * 2 + turn, i * 2 + group, i + it, ds(i * 4, 4))
                    turn, group = turn + 2 * size, group + 2 * size
                    if part < WHOLE_PARTS:
                        with act.Fori(0, DG // 2) as j2:
                            for b in range(2):
                                for s in range(SLOTS):
                                    split_hi(j2 * 2 + (turn + b + 1), s)
                                copy_tail(j2 * 2 + (group + b), j2 * (2 * SLOTS) + SLOTS * (turn + b + 1), 4 * b)
                for n, (j, kq) in enumerate(LAST_UNITS):
                    if turn + 1 + n // SLOTS < TURNS:
                        split_hi(turn + 1 + n // SLOTS, n % SLOTS)
                    if kq == LAST_PART - 1 and j == DG - 1:
                        if layer == 0:
                            act.wait_ge(banks_added, GROUP_FFN[1])
                            square_x(j, DG + j)
                            write_h_hi(range(4 * j, 4 * j + 4), KC)
                        else:
                            copy_out(2)
                    elif kq == LAST_PART - 1:
                        if layer == 1 and j == 2:
                            copy_out(0)
                            copy_out(1)
                        copy_tail(group + j, SLOTS * turn + n + 1, 4 * (j % 2))
                        if layer == 0:
                            act.wait_ge(x_added, X_LAST[0] + j + 1)
                            square_x(j, DG + j)
                            write_h_hi(range(4 * j, 4 * j + 4), KC)
                if layer == 0:
                    def finish(j):
                        act.wait_ge(x_added, X_POOL + j + 1)
                        write_h_hi(range(4 * j, 4 * j + 4), 3 * KC)

                    def scale_z(j):
                        act.wait_ge(units_done, SLOTS * TURN_POOL + j + 1)
                        for tt in range(TT):
                            last = nc.scalar.activation(z_rows[:, tt, j * UNIT_N:(j + 1) * UNIT_N], ps[:, 2 * j + tt, :],
                                                        ACT.Identity, scale=token_rstd[:, tt:tt + 1])
                        last.then_inc(z_ready, 1)

                    split_hi(TURN_POOL + 1, 0)
                    act.wait_ge(mixer_scale, RSQRT_STEPS)
                    scale_z(0)
                    scale_z(1)
                    split_hi(TURN_POOL + 1, 1)
                    finish(0)
                    scale_z(2)
                    split_hi(TURN_POOL + 1, 2)
                    finish(1)
                    scale_z(3)
                    split_hi(TURN_POOL + 1, 3)
                    finish(2)
                    finish(3)
                    for s in range(SLOTS):
                        split_hi(TURN_POOL + 2, s)
                    for j in range(DG):
                        square_x(j, 2 * DG + j)
            copy_out(DG - 1)

        @block.vector
        def _(dve):
            def split_lo(turn, slot):
                dve.wait_ge(hi_split, SLOTS * turn + (slot + 1))
                nc.vector.tensor_tensor(w_lo[:, slot], raw[:, slot], w_hi[:, slot].bitcast(F32), ALU.subtract).then_inc(lo_split, 1)

            def write_h_lo(j, gain_at, n):
                dve.wait_ge(h_hi_ready, n + 1)
                for k in range(4 * j, 4 * j + 4):
                    last = nc.vector.scalar_tensor_tensor(h_hl[:, k, T:2 * T], x_t[:, k, :], gains[:, gain_at + k:gain_at + k + 1],
                                                          h_hl[:, k, 0:T].bitcast(F32), ALU.mult, ALU.subtract)
                last.then_inc(h_ready, 1)

            def mean_rsqrt(total, count, v, r, done, at):
                n = [0]

                def then(ins):
                    n[0] += 1
                    ins.then_inc(done, 1)
                    dve.wait_ge(done, at + n[0])

                mean, t = v
                then(nc.vector.tensor_scalar(mean, total, 1.0 / count, EPS, ALU.mult, ALU.add))
                then(nc.vector.tensor_scalar(t.bitcast(I32), mean.bitcast(I32), 1, None, ALU.arith_shift_right))
                then(nc.vector.tensor_scalar(r.bitcast(I32), t.bitcast(I32), -1.0, float(RSQRT_SEED), ALU.mult, ALU.add))
                for _ in range(3):
                    then(nc.vector.scalar_tensor_tensor(t, r, -0.5, r, ALU.mult, ALU.mult))
                    then(nc.vector.tensor_tensor(t, t, mean, ALU.mult))
                    then(nc.vector.scalar_tensor_tensor(r, t, 1.5, r, ALU.add, ALU.mult))
                assert n[0] == RSQRT_STEPS

            nc.vector.memset(bias_rows[0:NH, :], MASKED).then_inc(bias_filled, 1)
            dve.wait_ge(gains_turned, 1)
            nc.vector.tensor_copy(gains[:], ps[:, 0, 0:5 * KC]).then_inc(gains_ready, 1)

            def copy_x(j):
                for i in (2 * j, 2 * j + 1):
                    dve.wait_ge(x_turned, i + 1)
                    nc.vector.tensor_copy(x_t[:, 2 * i:2 * i + 2, :].rearrange("p c t -> p (c t)"), ps[:, X_BANKS[i], :]).then_inc(x_copied, 1)

            copy_x(0)
            copy_x(1)
            dve.wait_ge(gains_ready, 1)
            for j in range(DG):
                write_h_lo(j, 0, j)
                split_lo(TURN_KV, j)
                if j + 2 < DG:
                    copy_x(j + 2)
            dve.wait_ge(table_landed, 32)
            nc.vector.transpose(table_t[0:NB, :], table[0:NH, :]).then_inc(table_turned, 1)
            dve.wait_ge(table_turned, 1)
            nc.vector.tensor_copy(table_p[0:NB, :].rearrange("b (q i o) -> b q i o", i=2, o=2),
                                  table_t[0:NB, :].rearrange("b (q o i) -> b q i o", i=2, o=2)).then_inc(table_turned, 1)
            dve.wait_ge(cols_landed, 16 * 5)
            nc.vector.tensor_scalar(q_gain_col[:], q_gain_col[:], DH ** -0.5, None, ALU.mult)
            nc.vector.tensor_scalar(neg_sink[:], sink[:], -1.0, None, ALU.mult).then_inc(sink_ready, 1)
            dve.wait_ge(ssq_done, TT)
            mean_rsqrt(token_ssq[:], D, (token_mean[:, 0], token_mean[:, 1]), token_rstd[:], rstd_ready, 0)
            split_lo(TURN_Q0, 0)
            split_lo(TURN_Q0, 1)
            for l in range(2):
                dve.wait_ge(params_turned, l + 1)
                nc.vector.tensor_copy(taps_early[:, l].rearrange("p k c -> p (k c)"), ps[:, 6 + l, 0:8 * FC]).then_inc(params_ready, 1)
            dve.wait_ge(bias_filled, 1)
            nc.vector.tensor_copy(bias_rows[0:NH, P:2 * P], ps[0:NH, 7, 8 * FC:8 * FC + P]).then_inc(bias_built, 1)
            split_lo(TURN_Q0, 2)
            split_lo(TURN_Q0, 3)

            for tt in range(TT):
                dve.wait_ge(kv_squared, tt + 1)
                nc.vector.tensor_reduce(head_ssq[:, tt, 0:NKV], probs[:, tt, :].rearrange("p (h d) -> p h d", h=NKV), AX.X, ALU.add).then_inc(kv_summed, 1)
            dve.wait_ge(kv_summed, TT)
            mean_rsqrt(head_ssq[:, :, 0:NKV], DH, (head_mean[:, 0, :, 0:NKV], head_mean[:, 1, :, 0:NKV]), head_rinv[:, :, 0:NKV], kv_rinv, 0)
            for tt in range(TT):
                rows = q_rows[:, tt, :].rearrange("p (h r d) -> p r h d", h=NKV, r=2)
                for r in range(2):
                    last = nc.vector.scalar_tensor_tensor(
                        rows[:, r], ps[:, 2 + tt, 0:NKV * DH].rearrange("p (h d) -> p h d", h=NKV), token_rstd[:, tt:tt + 1],
                        head_rinv[:, tt, 0:NKV].unsqueeze(2).broadcast_to([P, NKV, DH]), ALU.mult, ALU.mult)
                last.then_inc(k_rows_ready, 1)

            def copy_q(g, turn):
                dve.wait_ge(units_done, SLOTS * turn + SLOTS)
                nc.vector.tensor_scalar(q_rows[:, 1, :], ps[:, 1, :], token_rstd[:, 1:2], None, ALU.mult).then_inc(q_copied_dve, 1)

            def turned_q(g):
                dve.wait_ge(q_turned, 2 * g + 2)
                nc.vector.tensor_scalar(q_t[:, :, P:T], ps[:, 3, :].rearrange("p (c q) -> p c q", c=4),
                                        q_gain_col[:, 0:1], None, ALU.mult).then_inc(q_t_dve, 1)

            def sum_q(g):
                dve.wait_ge(q_squared, g + 1)
                nc.vector.tensor_reduce(head_ssq[:].rearrange("p t h -> p (t h)"), q_squares[:].rearrange("p t (h d) -> p (t h) d", h=8),
                                        AX.X, ALU.add).then_inc(q_summed, 1)

            def norm_q(g):
                dve.wait_ge(q_sums_turned, g + 1)
                mean_rsqrt(ps[:, 6, 0:8 * TT].rearrange("p (t h) -> p t h", t=TT), DH, (head_mean[:, 0], head_mean[:, 1]), head_rinv[:],
                           q_rinv, g * RSQRT_STEPS)

            for s in range(SLOTS - 1):
                split_lo(TURN_Q0 + 1, s)
            dve.wait_ge(k_turned, TT)
            copy_q(0, TURN_Q0)
            turned_q(0)
            sum_q(0)
            norm_q(0)
            split_lo(TURN_Q0 + 1, SLOTS - 1)

            def attend(g, turn, last):
                nc.vector.tensor_copy(v_group[:], v_rows[:, :, ds(g, 1) if not last else slice(g, g + 1), :]).then_inc(v_group_ready, 1)

                def bias_and_max(s):
                    half, tt = divmod(s, 2)
                    b, lo = s % 2, P * (1 - tt)
                    heads = (lambda t: t[:, ds(8 * g + 4 * half, 4)] if not last else t[:, 8 * g + 4 * half:8 * g + 4 * half + 4])
                    by_bank = (lambda t: t.rearrange("p (i o) -> p i o", i=2))
                    dve.wait_ge(scores_done, 4 * g + (s + 1))
                    dve.wait_ge(bias_landed[half], 16 * g + 16)
                    if s:
                        dve.wait_ge(probs_turned, 4 * g + s)
                    for j in range(4):
                        i, o = divmod(j, 2)
                        h = 4 * half + 2 * o + i
                        biased_last = nc.vector.scalar_tensor_tensor(probs[:, j, lo:], ps[:, 2 + i, 2 * P * o + lo:2 * P * (o + 1)],
                                                                 head_rinv[:, tt, h:h + 1], bias_ab[half][:, j, lo:], ALU.mult, ALU.add)
                    biased_last.then_inc(biased, 1)
                    dve.wait_ge(biased, 4 * g + (s + 1))
                    nc.vector.tensor_reduce(row_max[:, b, :], probs[:, :, lo:], AX.X, ALU.max).then_inc(maxed, 1)
                    dve.wait_ge(maxed, 4 * g + (s + 1))
                    nc.vector.scalar_tensor_tensor(by_bank(neg_max[:, b, :]), by_bank(row_max[:, b, :]), -1.0,
                                                   heads(neg_sink).rearrange("p (o i) -> p i o", i=2), ALU.mult, ALU.min).then_inc(neg_max_ready, 1)
                    dve.wait_ge(neg_max_ready, 4 * g + (s + 1))
                    nc.vector.tensor_tensor(by_bank(sink_arg[:, b, :]), by_bank(neg_max[:, b, :]),
                                            heads(sink).rearrange("p (o i) -> p i o", i=2), ALU.add).then_inc(sink_arg_ready, 1)

                def denominators(s):
                    b = s % 2
                    dve.wait_ge(exp_done, 4 * g + (s + 1))
                    nc.vector.tensor_tensor(row_den[:, b, :], row_sum[:, b, :], sink_exp[:, b, :], ALU.add).then_inc(den_ready, 1)
                    dve.wait_ge(den_ready, 4 * g + (s + 1))
                    nc.vector.reciprocal(row_rinv[:, b, :], row_den[:, b, :]).then_inc(rinv_ready, 1)

                def normalise_out(s):
                    b = s % 2
                    dve.wait_ge(pv_done, 4 * g + (s + 1))
                    dve.wait_ge(rinv_ready, 4 * g + (s + 1))
                    nc.vector.tensor_tensor(o_rows[:].rearrange("p (o i) d -> p o i d", i=2),
                                            ps[:, 6, 0:4 * DH].rearrange("p (o i d) -> p o i d", o=2, i=2),
                                            row_rinv[:, b, :].rearrange("p (i o) -> p o i", i=2).unsqueeze(3).broadcast_to([P, 2, 2, DH]),
                                            ALU.mult).then_inc(o_ready, 1)

                def out_lo(s):
                    half, tt = divmod(s, 2)
                    c0 = 4 * g + 2 * half
                    chunks = ds(c0, 2) if not last else slice(c0, c0 + 2)
                    dve.wait_ge(o_hi, 4 * g + (s + 1))
                    nc.vector.tensor_tensor(g_hl[:, chunks, T + tt * P:T + (tt + 1) * P], ps[:, 7, 0:2 * P].rearrange("p (c q) -> p c q", c=2),
                                            g_hl[:, chunks, tt * P:(tt + 1) * P].bitcast(F32), ALU.subtract).then_inc(o_lo, 1)

                bias_and_max(0)
                denominators(0)
                for s in range(4):
                    if s == 3 and not last:
                        copy_q(g + 1, turn)
                    if s:
                        out_lo(s - 1)
                    if s % 2:
                        dve.wait_ge(probs_turned, 4 * g + (s + 1))
                        nc.vector.tensor_copy(probs_t[:, 1], ps[:, 5, :].rearrange("p (h q) -> p h q", h=4)).then_inc(probs_t_dve, 1)
                    if s < 3:
                        bias_and_max(s + 1)
                    elif not last:
                        turned_q(g + 1)
                        sum_q(g + 1)
                    normalise_out(s)
                    if s < 3 and not last:
                        split_lo(turn + 1, s)
                    if s in (1, 2) and last:
                        split_lo(turn + 1, s - 1)
                    if s < 3:
                        denominators(s + 1)
                out_lo(3)
                if not last:
                    norm_q(g + 1)
                if last:
                    split_lo(turn + 1, 2)
                split_lo(turn + 1, 3)

            dve.wait_ge(sink_ready, 1)
            with dve.Fori(0, NKV - 1) as g:
                attend(g, TURN_Q0 + 1 + g, False)
            attend(NKV - 1, TURN_WO, True)

            def sum_squares(n):
                dve.wait_ge(squared, n + 1)
                if n == DG:
                    dve.wait_ge(ssq_all_ready, 1)
                if n == 2 * DG:
                    dve.wait_ge(token_sums_turned, 1)
                if n % DG >= 2:
                    dve.wait_ge(ssq_local_ready, (DG - 1) * (n // DG) + n % DG - 1)
                nc.vector.tensor_reduce((ssq_part if n % DG else ssq_local)[:], squares_for(n)[:].rearrange("p c t -> p t c"), AX.X, ALU.add).then_inc(ssq_reduced, 1)
                if n % DG:
                    dve.wait_ge(ssq_reduced, n + 1)
                    nc.vector.tensor_tensor(ssq_local[:], ssq_local[:], ssq_part[:], ALU.add).then_inc(ssq_local_ready, 1)

            def token_rsqrt(n):
                dve.wait_ge(ssq_all_ready, n + 1)
                mean_rsqrt(ssq_all[:], D, (ssq_mean[:, 0], ssq_mean[:, 1]), rstd[:], token_scale, n * RSQRT_STEPS)

            for j in range(DG):
                if j:
                    for s in range(SLOTS):
                        split_lo(TURN_WO + j + 1, s)
                dve.wait_ge(units_done, SLOTS * (TURN_WO + j + 1))
                x_group = x_t[:, 4 * j:4 * j + 4, :].rearrange("p c t -> p (c t)")
                nc.vector.tensor_tensor(x_group, x_group, ps[:, 2 * j:2 * j + 2, :].rearrange("p b n -> p (b n)"), ALU.add).then_inc(banks_added, 1)
                dve.wait_ge(banks_added, j + 1)
                sum_squares(j)
                write_h_lo(j, 2 * KC, DG + j)
            token_rsqrt(0)
            dve.wait_ge(taps_landed, 16)

            def add_banks(layer, group, banks):
                dve.wait_ge(tail_copied, group + (1 - DG - layer))
                nc.vector.tensor_tensor(pre[:], ps[:, banks:banks + 4, 0:T], tail[:], ALU.add).then_inc(banks_added, 1)
                dve.wait_ge(banks_added, group + 1)

            def conv(layer, group, banks, n, y, chunk0, norm=None):
                if banks:
                    dve.wait_ge(conv_done, n)
                add_banks(layer, group, banks)
                if norm is not None:
                    token_rsqrt(norm)
                nc.vector.tensor_tensor(pre[:], pre[:], rstd[:].unsqueeze(1).broadcast_to([P, 4, T]), ALU.mult).then_inc(pre_scaled, 1)
                dve.wait_ge(pre_scaled, n + 1)

                def tap(k, c):
                    return taps[:, layer, k, ds(chunk0 + c, 1)]

                for c in range(4):
                    last = nc.vector.tensor_scalar(y[:, c, :], pre[:, c, :], tap(2, c), tap(3, c), ALU.mult, ALU.add)
                last.then_inc(tap_mid, 1)
                dve.wait_ge(tap_mid, n + 1)
                for c in range(4):
                    last = nc.vector.scalar_tensor_tensor(y[:, c, 1:T], pre[:, c, 0:T - 1], tap(1, c), y[:, c, 1:T], ALU.mult, ALU.add)
                last.then_inc(tap_prev, 1)
                dve.wait_ge(tap_prev, n + 1)
                for c in range(4):
                    last = nc.vector.scalar_tensor_tensor(y[:, c, 2:T], pre[:, c, 0:T - 2], tap(0, c), y[:, c, 2:T], ALU.mult, ALU.add)
                last.then_inc(conv_done, 1)

            def gate_values(it, chunks):
                dve.wait_ge(conv_done, 2 * it + 2)
                dve.wait_ge(silu_done, it + 1)
                nc.vector.tensor_tensor(y_val[:], y_val[:], y_gate[:], ALU.mult).then_inc(gated, 1)
                dve.wait_ge(g_hi, it + 1)
                nc.vector.tensor_tensor(g_hl[:, chunks, T:2 * T], y_val[:], g_hl[:, chunks, 0:T].bitcast(F32), ALU.subtract).then_inc(g_lo, 1)

            def mlp_group(layer, turn, group, it, chunks, chunk0, split=0):
                for s in range(split, SLOTS):
                    split_lo(turn + 1, s)
                conv(layer, group, 0, 2 * it, y_gate, chunk0)
                for s in range(SLOTS):
                    split_lo(turn + 2, s)
                conv(layer, group + 1, 4, 2 * it + 1, y_val, chunk0 + FC)
                gate_values(it, chunks)

            def first_mlp_group(layer, turn, group, it):
                split_lo(turn + 2, 0)
                split_lo(turn + 2, 1)
                conv(layer, group, 0, 2 * it, y_gate, 0, norm=1)
                split_lo(turn + 2, 2)
                split_lo(turn + 2, 3)
                conv(layer, group + 1, 4, 2 * it + 1, y_val, FC)
                split_lo(turn + 3, 0)
                split_lo(turn + 3, 1)
                gate_values(it, slice(0, 4))

            def add_last_to_x(layer):
                dve.wait_ge(units_done, SLOTS * (TURN_FFN[layer] + FFN_TURNS))
                x_group = x_t[:, 4 * (DG - 1):4 * DG, :].rearrange("p c t -> p (c t)")
                nc.vector.tensor_tensor(x_group, x_group, ps[:, 4:6, :].rearrange("p b n -> p (b n)"), ALU.add).then_inc(banks_added, 1)
                dve.wait_ge(banks_added, GROUP_FFN[layer] + FFN_GROUPS)

            def add_to_x(layer, group, banks, chunks, x_steps):
                add_banks(layer, group, banks)
                x_group = x_t[:, chunks, :]
                nc.vector.tensor_tensor(x_group, x_group, pre[:], ALU.add).then_inc(x_added, 1)
                dve.wait_ge(x_added, x_steps)

            for layer in range(2):
                for part, size in enumerate(PARTS):
                    turn, group, it = part_start(layer, part)
                    if (layer, part) == (1, 0):
                        first_mlp_group(layer, turn, group, it)
                        mlp_group(layer, turn + 2, group + 2, it + 1, slice(4, 8), 4, split=2)
                    with dve.Fori(first_in_loop(layer, part), size) as i:
                        mlp_group(layer, i * 2 + turn, i * 2 + group, i + it, ds(i * 4, 4), i * 4 + part * KC)
                    turn, group = turn + 2 * size, group + 2 * size
                    if part < WHOLE_PARTS:
                        with dve.Fori(0, DG // 2) as j2:
                            for b in range(2):
                                for s in range(SLOTS):
                                    split_lo(j2 * 2 + (turn + b + 1), s)
                                add_to_x(layer, j2 * 2 + (group + b), 4 * b, ds(j2 * 8 + 4 * b, 4), j2 * 2 + (X_FFN[layer] + part * DG + b + 1))
                for n, (j, kq) in enumerate(LAST_UNITS):
                    if kq == LAST_PART - 1 and j == DG - 1:
                        add_last_to_x(layer)
                        if layer == 0:
                            sum_squares(DG + j)
                            split_lo(turn + 1 + n // SLOTS, n % SLOTS)
                            write_h_lo(j, KC, 2 * DG + j)
                        continue
                    if turn + 1 + n // SLOTS < TURNS:
                        split_lo(turn + 1 + n // SLOTS, n % SLOTS)
                    if kq == LAST_PART - 1:
                        add_to_x(layer, group + j, 4 * (j % 2), slice(4 * j, 4 * j + 4), X_LAST[layer] + j + 1)
                        if layer == 0:
                            sum_squares(DG + j)
                            write_h_lo(j, KC, 2 * DG + j)
                if layer == 1:
                    continue

                dve.wait_ge(token_sums_turned, 1)
                mean_rsqrt(ps[:, 7, 0:TT], D, (token_mean[:, 0], token_mean[:, 1]), token_rstd[:], mixer_scale, 0)

                def add_pooled(j):
                    dve.wait_ge(pooled, j + 1)
                    for c in range(4):
                        k = 4 * j + c
                        last = nc.vector.scalar_tensor_tensor(x_t[:, k, :], ps[:, 2 * j + c // 2, (c % 2) * T:(c % 2 + 1) * T],
                                                              gains[:, 4 * KC + k:4 * KC + k + 1], x_t[:, k, :], ALU.mult, ALU.add)
                    last.then_inc(x_added, 1)
                    dve.wait_ge(x_added, X_POOL + j + 1)

                split_lo(TURN_POOL + 1, 0)
                for j in range(DG):
                    add_pooled(j)
                    if j < DG - 1:
                        split_lo(TURN_POOL + 1, j + 1)
                    write_h_lo(j, 3 * KC, 3 * DG + j)
                for s in range(SLOTS):
                    split_lo(TURN_POOL + 2, s)
                for j in range(DG):
                    sum_squares(2 * DG + j)

        @block.tensor
        def _(pe):
            pe.wait_ge(ident_ready, 2)
            pe.wait_ge(gains_landed, 16 * 3)
            nc.tensor.transpose(ps[:, 0, 0:5 * KC], gain_rows[0:5 * KC, :], ident[0:5 * KC, 0:5 * KC]).then_inc(gains_turned, 1)

            def turn_in(j):
                pe.wait_ge(x_landed[j], 16)
                for i in (2 * j, 2 * j + 1):
                    if i >= 5:
                        pe.wait_ge(x_copied, i - 4)
                    for c in range(2):
                        for tt in range(TT):
                            last = nc.tensor.transpose(ps[:, X_BANKS[i], c * T + tt * P:c * T + (tt + 1) * P],
                                                       x_rows[:, tt, (2 * i + c) * P:(2 * i + c + 1) * P], ident[:])
                    last.then_inc(x_turned, 1)

            def turn_params():
                pe.wait_ge(params_landed, 16 * 3)
                pe.wait_ge(x_copied, 5)
                for l in range(2):
                    if l == 1:
                        pe.wait_ge(table_turned, 2)
                        nc.tensor.matmul(ps[0:NH, 7, 8 * FC:8 * FC + P], table_p[0:NB, :], onehot[0:NB, :], start=True, stop=True)
                    for k in range(4):
                        last = nc.tensor.transpose(ps[:, 6 + l, k * 2 * FC:(k + 1) * 2 * FC], conv_rows[0:2 * FC, l, k, :],
                                                   ident[0:2 * FC, 0:2 * FC])
                    last.then_inc(params_turned, 1)

            def turn_x(j):
                if j < DG - 1:
                    pe.wait_ge(x_added, X_LAST[1] + max(j, 1) + 1)
                else:
                    pe.wait_ge(banks_added, GROUP_FFN[1] + FFN_GROUPS)
                for tt in range(TT):
                    for c in range(4):
                        last = nc.tensor.transpose(ps[:, OUT_BANKS[j] + tt, c * P:(c + 1) * P], x_t[:, 4 * j + c, tt * P:(tt + 1) * P], ident[:])
                last.then_inc(out_turned, 1)

            def rows_chunk(turn, c, bank0):
                slot, k = divmod(c, UNIT_K)
                if k == 0:
                    pe.wait_ge(lo_split, SLOTS * turn + (slot + 1))
                for tt in range(TT):
                    a_hi, a_lo = h_hl[:, c, tt * P:(tt + 1) * P], h_hl[:, c, T + tt * P:T + (tt + 1) * P]
                    o = ps[:, bank0 + tt, :]
                    nc.tensor.matmul(o, a_hi, w_hi[:, slot, k, :], start=(c == 0), stop=False)
                    nc.tensor.matmul(o, a_hi, w_lo[:, slot, k, :], start=False, stop=False)
                    last = nc.tensor.matmul(o, a_lo, w_hi[:, slot, k, :], start=False, stop=(c == KC - 1))
                if k == UNIT_K - 1:
                    last.then_inc(units_done, 1)

            def rows_unit(turn, kq, bank0):
                for k in range(UNIT_K):
                    rows_chunk(turn, 4 * kq + k, bank0)

            def narrow_chunk(turn, slot, k, act_hl, chunk, bank0, first, ended):
                if k == 0:
                    pe.wait_ge(lo_split, SLOTS * turn + (slot + 1))
                for c in range(4):
                    o = ps[:, bank0 + c // 2, (c % 2) * T:(c % 2 + 1) * T]
                    hi, lo = w_hi[:, slot, k, c * P:(c + 1) * P], w_lo[:, slot, k, c * P:(c + 1) * P]
                    clears = first and c % 2 == 0
                    nc.tensor.matmul(o, hi, act_hl[:, chunk, 0:T], start=clears, stop=False, skip_group_check=True)
                    nc.tensor.matmul(o, hi, act_hl[:, chunk, T:2 * T], start=False, stop=False, skip_group_check=True)
                    last = nc.tensor.matmul(o, lo, act_hl[:, chunk, 0:T], start=False, stop=ended, skip_group_check=True)
                if k == UNIT_K - 1:
                    last.then_inc(units_done, 1)

            def wo_chunk(turn, c, bank0):
                narrow_chunk(turn, c // UNIT_K, c % UNIT_K, g_hl, c, bank0, c == 0, c == KC - 1)

            def unit(turn, slot, act_hl, chunk0, banks, first, ended):
                pe.wait_ge(lo_split, SLOTS * turn + (slot + 1))
                for k in range(4):
                    for c in range(4):
                        hi, lo = w_hi[:, slot, k, c * P:(c + 1) * P], w_lo[:, slot, k, c * P:(c + 1) * P]
                        both, left = ps[:, banks + c, :], ps[:, banks + c, 0:T]
                        a_both, a_hi = act_hl[:, chunk0 + k, :], act_hl[:, chunk0 + k, 0:T]
                        if ended and k == 3:
                            nc.tensor.matmul(left, lo, a_hi, start=False, stop=False)
                            last = nc.tensor.matmul(both, hi, a_both, start=False, stop=True)
                        else:
                            nc.tensor.matmul(both, hi, a_both, start=(first and k == 0), stop=False)
                            last = nc.tensor.matmul(left, lo, a_hi, start=False, stop=False)
                last.then_inc(units_done, 1)

            turn_in(0)
            turn_in(1)
            for kq in range(4):
                if kq < 2:
                    turn_in(kq + 2)
                pe.wait_ge(h_ready, kq + 1)
                rows_unit(TURN_KV, kq, 2)
            turn_params()
            for kq in range(4):
                if kq == 3:
                    for tt in range(TT):
                        pe.wait_ge(k_rows_ready, tt + 1)
                        for h in range(NKV):
                            last = nc.tensor.transpose(ps[:, 4 + tt, h * P:(h + 1) * P], q_rows[:, tt, h * P:(h + 1) * P], ident[:])
                        last.then_inc(k_turned, 1)
                rows_unit(TURN_Q0, kq, 0)

            def turn_q(g):
                for tt in range(TT):
                    pe.wait_ge(q_copied_act if tt == 0 else q_copied_dve, g + 1)
                    for c in range(4):
                        last = nc.tensor.matmul(ps[:, 2 + tt, c * P:(c + 1) * P], q_rows[:, tt, c * P:(c + 1) * P], mirror[:], start=True, stop=True)
                    last.then_inc(q_turned, 1)

            def turn_q_sums(g):
                pe.wait_ge(q_summed, g + 1)
                nc.tensor.matmul(ps[:, 6, 0:8 * TT], mirror[:], head_ssq[:].rearrange("p t h -> p (t h)"), start=True, stop=True).then_inc(q_sums_turned, 1)

            def scores(g, s):
                half, tt = divmod(s, 2)
                if s == 0:
                    pe.wait_ge(k_group_ready, g + 1)
                    pe.wait_ge(q_t_act, g + 1)
                    pe.wait_ge(q_t_dve, g + 1)
                else:
                    pe.wait_ge(biased, 4 * g + s)
                for a in range(4):
                    r, i, o = DH * (a % 2), a % 2, a // 2
                    out_cols = slice(2 * P * o + P * (1 - tt), 2 * P * (o + 1))
                    last = nc.tensor.matmul(ps[:, 2 + i, out_cols], q_t[r:r + DH, 2 * half + o, tt * P:(tt + 1) * P],
                                            k_group[r:r + DH, 0, 0:P * (tt + 1)], start=True, stop=True)
                last.then_inc(scores_done, 1)

            def attend(g, turn, run_chunk, last_group):
                def turn_probs(s):
                    pe.wait_ge(exp_done, 4 * g + (s + 1))
                    if s:
                        pe.wait_ge(probs_t_act, 4 * g + s)
                    if s >= 2:
                        pe.wait_ge(probs_t_dve, 2 * g + s // 2)
                    for kb in range(1 - s % 2, 2):
                        for j in range(4):
                            last = nc.tensor.transpose(ps[:, 4 + kb, j * P:(j + 1) * P], probs[:, j, kb * P:(kb + 1) * P], ident[:])
                    last.then_inc(probs_turned, 1)

                def values(s):
                    tt = s % 2
                    pe.wait_ge(v_group_ready, g + 1)
                    pe.wait_ge(probs_t_act, 4 * g + (s + 1))
                    if s:
                        pe.wait_ge(probs_t_dve, 2 * g + (s + 1) // 2)
                        pe.wait_ge(o_ready, 4 * g + s)
                    for a in range(4):
                        j = (a % 2) * 2 + a // 2
                        for kb in range(1 - tt, 2):
                            last = nc.tensor.matmul(ps[:, 6, a * DH:(a + 1) * DH], probs_t[:, kb, j, :],
                                                    v_group[:, kb if tt else 0, 0, :], start=(kb == 1 - tt), stop=(kb == 1))
                    last.then_inc(pv_done, 1)

                def turn_out(s):
                    pe.wait_ge(o_ready, 4 * g + (s + 1))
                    if s:
                        pe.wait_ge(o_lo, 4 * g + s)
                    for c in range(2):
                        last = nc.tensor.matmul(ps[:, 7, c * P:(c + 1) * P],
                                                o_rows[:, 2 * c:2 * c + 2, :].rearrange("p a d -> p (a d)"), mirror[:], start=True, stop=True)
                    last.then_inc(o_turned, 1)

                steps = LAST_STEP_CHUNKS if last_group else STEP_CHUNKS
                for s in range(4):
                    for c in range(steps[s], steps[s + 1]):
                        run_chunk(turn, c)
                    if s:
                        turn_out(s - 1)
                    turn_probs(s)
                    if s < 3:
                        scores(g, s + 1)
                    elif not last_group:
                        pe.wait_ge(biased, 4 * g + 4)
                        turn_q(g + 1)
                    values(s)
                if not last_group:
                    scores(g + 1, 0)
                turn_out(3)
                if not last_group:
                    turn_q_sums(g + 1)
                if last_group:
                    pe.wait_ge(o_lo, 4 * g + 4)
                    for c in range(steps[4], KC):
                        run_chunk(turn, c)

            def q_chunk(turn, c):
                if c == 0:
                    pe.wait_ge(q_squared, turn - TURN_Q0)
                rows_chunk(turn, c, 0)

            def first_wo_chunk(turn, c):
                if c == 0:
                    pe.wait_ge(q_squared, NKV)
                wo_chunk(turn, c, 0)

            turn_q(0)
            turn_q_sums(0)
            scores(0, 0)
            with pe.Fori(0, NKV - 1) as g:
                attend(g, TURN_Q0 + 1 + g, q_chunk, False)
            attend(NKV - 1, TURN_WO, first_wo_chunk, True)
            for j in range(1, DG):
                for c in range(KC):
                    wo_chunk(TURN_WO + j, c, 2 * j)

            def mlp_group(turn, group, h_steps):
                for half in range(2):
                    pe.wait_ge(banks_added, group + (half - 1))
                    for kq in range(4):
                        pe.wait_ge(h_ready, h_steps + kq + 1)
                        unit(turn + half, kq, h_hl, 4 * kq, 4 * half, kq == 0, kq == 3)

            def first_mlp_group(turn, group, h_steps):
                for n, (half, kq) in enumerate(FIRST_UNITS):
                    if kq == 0:
                        pe.wait_ge(x_added, X_POOL + 2 + 2 * half)
                    pe.wait_ge(h_ready, h_steps + kq + 1)
                    unit(turn + n // SLOTS, n % SLOTS, h_hl, 4 * kq, 4 * half, kq == 0, kq == 3)

            for layer in range(2):
                h_steps = DG if layer == 0 else 3 * DG
                for part, size in enumerate(PARTS):
                    turn, group, it = part_start(layer, part)
                    if (layer, part) == (1, 0):
                        first_mlp_group(turn, group, h_steps)
                        mlp_group(turn + 2, group + 2, h_steps)
                    with pe.Fori(first_in_loop(layer, part), size) as i:
                        mlp_group(i * 2 + turn, i * 2 + group, h_steps)
                    turn, group = turn + 2 * size, group + 2 * size
                    if part < WHOLE_PARTS:
                        with pe.Fori(0, DG // 2) as j2:
                            for b in range(2):
                                pe.wait_ge(banks_added, j2 * 2 + (group + b - 1))
                                for kq in range(PART):
                                    pe.wait_ge(g_lo, it + kq + 1)
                                    unit(j2 * 2 + (turn + b), kq, g_hl, 4 * kq, 4 * b, kq == 0, kq == PART - 1)
                for n, (j, kq) in enumerate(LAST_UNITS):
                    if kq == 0:
                        pe.wait_ge(banks_added, group + j - 1)
                        if layer == 1 and j == 3:
                            pe.wait_ge(out_copied, 2)
                    pe.wait_ge(g_lo, it + kq + 1)
                    if j == DG - 1:
                        for k in range(UNIT_K):
                            narrow_chunk(turn + n // SLOTS, n % SLOTS, k, g_hl, 4 * kq + k, 4,
                                         kq == 0 and k == 0, kq == LAST_PART - 1 and k == UNIT_K - 1)
                    else:
                        unit(turn + n // SLOTS, n % SLOTS, g_hl, 4 * kq, 4 * (j % 2), kq == 0, kq == LAST_PART - 1)
                    if layer == 1 and (j, kq) == (2, 1):
                        turn_x(0)
                        turn_x(1)
                    if layer == 1 and (j, kq) == (3, 1):
                        turn_x(2)
                if layer == 0:
                    def pool_tokens(j):
                        pe.wait_ge(z_ready, j + 1)
                        for c in range(4):
                            o, f = ps[:, 2 * j + c // 2, :], slice(j * UNIT_N + c * P, j * UNIT_N + (c + 1) * P)
                            left = (c % 2) * T
                            nc.tensor.matmul(o[:, left:left + P + MAP_REACH], z_rows[:, 0, f], pool_map[:, j, 0:P + MAP_REACH],
                                             start=(c % 2 == 0), stop=False, skip_group_check=True)
                            last = nc.tensor.matmul(o[:, left + P:left + T], z_rows[:, 1, f], pool_map[:, j, P + MAP_REACH:],
                                                    start=False, stop=True, skip_group_check=True)
                        last.then_inc(pooled, 1)

                    for j in range(DG):
                        pe.wait_ge(banks_added, GROUP_FFN[1] - (j < 2))
                        pe.wait_ge(h_ready, 2 * DG + j + 1)
                        pe.wait_ge(lo_split, SLOTS * TURN_POOL + j + 1)
                        for k in range(UNIT_K):
                            for tt in range(TT):
                                a_hi = h_hl[:, 4 * j + k, tt * P:(tt + 1) * P]
                                a_lo = h_hl[:, 4 * j + k, T + tt * P:T + (tt + 1) * P]
                                o = ps[:, 2 * j + tt, :]
                                nc.tensor.matmul(o, a_hi, w_hi[:, j, k, :], start=(k == 0), stop=False)
                                nc.tensor.matmul(o, a_hi, w_lo[:, j, k, :], start=False, stop=False)
                                last = nc.tensor.matmul(o, a_lo, w_hi[:, j, k, :], start=False, stop=(k == UNIT_K - 1))
                        last.then_inc(units_done, 1)
                        if j == 0:
                            pe.wait_ge(ssq_local_ready, (DG - 1) * 2)
                            for tt in range(TT):
                                last = nc.tensor.matmul(ps[:, 7, tt:tt + 1], ssq_local[:, tt * P:(tt + 1) * P], ones[:], start=True, stop=True)
                            last.then_inc(token_sums_turned, 1)
                            pe.wait_ge(pool_map_landed, 16)
                        else:
                            pool_tokens(j - 1)
                    pool_tokens(DG - 1)
            turn_x(DG - 1)


_INS = ["x", "norm_mix", "norm_ffn", "rel_bias", "attn_w_qkv", "attn_q_gain", "attn_k_gain", "attn_sinks", "attn_w_o",
        "pool_w", "pool_scale", "ffn_w_up", "ffn_conv_w", "ffn_conv_b", "ffn_w_down"]


def _bucket_onehot(n_buckets, window, max_distance=128):
    import numpy as np
    n = np.arange(window)[::-1]
    exact = n_buckets // 2
    nf = np.maximum(n, 1).astype(np.float32)
    large = exact + (np.log(nf / exact) / np.log(max_distance / exact) * (n_buckets - exact)).astype(np.int32)
    bucket = np.where(n < exact, n, np.minimum(large, n_buckets - 1))
    return (np.arange(n_buckets)[:, None] == bucket[None, :]).astype(np.float32)


def _pool_maps(windows):
    import numpy as np
    t_in, t_out = np.arange(2 * P)[:, None], np.arange(2 * P)[None, :]
    maps = []
    for w in windows:
        inside = (t_in <= t_out) & (t_out - t_in < w)
        m = inside / np.minimum(t_out + 1, w) - (t_in == t_out)
        maps.append(np.concatenate([m[:P, :P + MAP_REACH], m[P:, P:]], axis=1))
    return np.stack(maps, axis=1).reshape(P, -1).astype(np.float32)


def kernel(**inputs):
    import numpy as np
    from concourse import bacc
    from concourse.bass_utils import run_bass_kernel_spmd

    nc = bacc.Bacc("TRN2", target_bir_lowering=False, num_devices=1)
    given = {name: np.ascontiguousarray(inputs[name]) for name in _INS}
    given["bucket_onehot"] = _bucket_onehot(given["rel_bias"].shape[1], 128)
    given["pool_maps"] = _pool_maps(POOL_WINDOWS)
    arrays, args = {}, []
    for name, a in given.items():
        arrays[f"in_{name}"] = a
        args.append(nc.dram_tensor(f"in_{name}", a.shape, mybir.dt.from_np(a.dtype), kind="ExternalInput").ap())
    out = nc.dram_tensor("out", given["x"].shape, F32, kind="ExternalOutput").ap()
    build_trunk(nc, *args, out)
    return run_bass_kernel_spmd(nc, [arrays], core_ids=[0]).results[0]["out"]
```
